# Optimizing a Trainium2 kernel written in Bass

```python
import jax, jax.numpy as jnp
from jax import lax
import numpy as np

D_MODEL = 2048
BATCH = 1
SEQ = 256
DEPTH = 2
DEC_BATCH = 8
DEC_SEQ = 1
PAST_LEN = 2048
PAGE_SIZE = 128

N_A = DEPTH // 2
N_B = DEPTH - N_A
MEM_TOKENS = 256
N_MEM_HEADS = 4
MEM_HEAD_DIM = 128
MEM_W = N_MEM_HEADS * MEM_HEAD_DIM
MIX_W = D_MODEL
MAIN_W = MIX_W - MEM_W
POOL_WINDOWS = (2, 4, 8, 16)
POOL_GC = MAIN_W // len(POOL_WINDOWS)
POOL_BUF = max(POOL_WINDOWS) - 1
HEAD_DIM = 128
N_HEADS = MAIN_W // HEAD_DIM
N_KV = 4
GQA = N_HEADS // N_KV
N_BRANCH = 3
GATE_W = N_HEADS * N_BRANCH
CMP_BLOCK = 32
CMP_STRIDE = 16
CMP_HIDDEN = HEAD_DIM
SLC_BLOCK = 64
N_SELECT = 16
WINDOW = 512
Q_BLOCK = 128
D_FF = -(-(8 * D_MODEL) // (3 * 256)) * 256
ROPE_THETA = 10000.0
EPS = 1e-6
NEG = -1e30
F32 = jnp.float32
SCALE = HEAD_DIM ** -0.5
MEM_SCALE = MEM_HEAD_DIM ** -0.5

kernel_name = 'yoco_pool_nsa_memory_decoder_step'

def rmsnorm(x, g):
    xf = x.astype(F32)
    y = xf * lax.rsqrt(jnp.mean(xf * xf, -1, keepdims=True) + EPS)
    return (y * g.astype(F32)).astype(x.dtype)

def rope(x, pos):
    half = HEAD_DIM // 2
    inv = ROPE_THETA ** (-jnp.arange(half, dtype=F32) / half)
    ang = pos.astype(F32)[:, None] * inv[None, :]
    cos = jnp.cos(ang)[None, :, None, :]
    sin = jnp.sin(ang)[None, :, None, :]
    xf = x.astype(F32)
    x1, x2 = xf[..., :half], xf[..., half:]
    return jnp.concatenate([x1 * cos - x2 * sin, x2 * cos + x1 * sin], -1).astype(x.dtype)

def pad_seq(x, mult):
    pad = (-x.shape[1]) % mult
    return jnp.pad(x, [(0, 0), (0, pad)] + [(0, 0)] * (x.ndim - 2))

def swiglu(h, w_gu, w_down):
    a, b = jnp.split(h @ w_gu, 2, axis=-1)
    return (jax.nn.silu(a) * b) @ w_down

def causal_pool_mix(p, buf, pos, w_grp, scale):
    S = p.shape[1]
    full = jnp.concatenate([buf.astype(p.dtype), p], 1)
    ff = full.astype(F32)
    cs = jnp.concatenate([jnp.zeros_like(ff[:, :1]), lax.cumsum(ff, axis=1)], 1)
    outs = []
    for g, w in enumerate(POOL_WINDOWS):
        sl = slice(g * POOL_GC, (g + 1) * POOL_GC)
        win_sum = cs[:, POOL_BUF + 1:POOL_BUF + 1 + S, sl] - cs[:, POOL_BUF + 1 - w:POOL_BUF + 1 - w + S, sl]
        cnt = jnp.minimum(pos + 1, w).astype(F32)[None, :, None]
        d = win_sum / cnt - ff[:, POOL_BUF:, sl]
        outs.append(jnp.einsum('bsc,cd->bsd', d, w_grp[g].astype(F32)))
    z = jnp.concatenate(outs, -1) * scale.astype(F32)
    return z.astype(p.dtype), full[:, -POOL_BUF:]

def mem_kv_proj(mem, g, w):
    B, M = mem.shape[:2]
    return (rmsnorm(mem, g) @ w).reshape(B, M, 2, N_MEM_HEADS, MEM_HEAD_DIM)

def mem_attend(qm, mkv):
    s = jnp.einsum('bshd,bmhd->bhsm', qm.astype(F32), mkv[:, :, 0].astype(F32)) * MEM_SCALE
    p = jax.nn.softmax(s, axis=-1)
    o = jnp.einsum('bhsm,bmhd->bshd', p, mkv[:, :, 1].astype(F32))
    return o.reshape(qm.shape[0], qm.shape[1], MEM_W).astype(qm.dtype)

def shared_kv(x, pos, g_kv, w_kv):
    B, S, _ = x.shape
    kv = (rmsnorm(x, g_kv) @ w_kv).reshape(B, S, N_BRANCH, 2, N_KV, HEAD_DIM)
    return [jnp.stack([rope(kv[:, :, br, 0], pos), kv[:, :, br, 1]], 2) for br in range(N_BRANCH)]

def compress(kv, cmp_pe, cmp_w1, cmp_w2):
    B, T = kv.shape[:2]
    n_ch = T // CMP_STRIDE
    ch = kv.reshape(B, n_ch, CMP_STRIDE, 2, N_KV, HEAD_DIM)
    w1 = cmp_w1.reshape(2, 2, CMP_STRIDE, HEAD_DIM, CMP_HIDDEN)
    pe = cmp_pe.reshape(2, 2, CMP_STRIDE, HEAD_DIM)

    def half(i):
        return (jnp.einsum('bnrchd,crdf->bnchf', ch, w1[:, i], preferred_element_type=F32)
                + jnp.einsum('crd,crdf->cf', pe[:, i], w1[:, i]).astype(F32)[None, None, :, None, :])

    hid = jax.nn.gelu(half(0)[:, :-1] + half(1)[:, 1:])
    out = jnp.einsum('bnchf,cfd->bnchd', hid, cmp_w2.astype(F32))
    ends = jnp.arange(n_ch - 1) * CMP_STRIDE + CMP_BLOCK - 1
    return out, ends

def cmp_attend(q, ckv, ends, qpos):
    s = jnp.einsum('bqhgd,bnhd->bqhgn', q.astype(F32), ckv[:, :, 0]) * SCALE
    vis = ends[None, :] <= qpos[:, None]
    s = jnp.where(vis[None, :, None, None, :], s, NEG)
    p = jax.nn.softmax(s, axis=-1) * jnp.any(vis, -1).astype(F32)[None, :, None, None, None]
    o = jnp.einsum('bqhgn,bnhd->bqhgd', p, ckv[:, :, 1])
    return o, p

def select_blocks(p_cmp, ends, qpos, n_slc):
    starts = ends - (CMP_BLOCK - 1)
    jst = jnp.arange(n_slc) * SLC_BLOCK
    cover = ((starts[:, None] < jst[None, :] + SLC_BLOCK) & (ends[:, None] >= jst[None, :])).astype(F32)
    score = jnp.einsum('bqhgn,nj->bqhj', p_cmp, cover)
    qb = (qpos // SLC_BLOCK)[:, None]
    jidx = jnp.arange(n_slc)[None, :]
    valid = jidx <= qb
    forced = (jidx == 0) | (jidx == qb) | (jidx == qb - 1)
    score = jnp.where(forced[None, :, None, :], jnp.inf,
                      jnp.where(valid[None, :, None, :], score, -jnp.inf))
    _, idx = lax.top_k(score, min(N_SELECT, n_slc))
    return idx.astype(jnp.int32)

def gathered_attend(q, kg, vg, kpos, qpos):
    s = jnp.einsum('...hgd,...hkd->...hgk', q.astype(F32), kg.astype(F32)) * SCALE
    vis = kpos[..., :, None, :] <= qpos[..., None, None, None]
    p = jax.nn.softmax(jnp.where(vis, s, NEG), axis=-1)
    return jnp.einsum('...hgk,...hkd->...hgd', p, vg.astype(F32))

def slc_prompt(q, slc_kv, sel, pos):
    B, S = q.shape[:2]
    nb = slc_kv.shape[1] // SLC_BLOCK
    n_sel = sel.shape[-1]
    blocks = slc_kv.reshape(B, nb, SLC_BLOCK, 2, N_KV, HEAD_DIM).transpose(0, 3, 4, 1, 2, 5)
    nqb = S // Q_BLOCK
    qs = q.reshape(B * nqb, Q_BLOCK, N_KV, GQA, HEAD_DIM)
    ss = sel.reshape(B * nqb, Q_BLOCK, N_KV, n_sel)
    ps = jnp.broadcast_to(pos.reshape(1, nqb, Q_BLOCK), (B, nqb, Q_BLOCK)).reshape(B * nqb, Q_BLOCK)
    bs = jnp.repeat(jnp.arange(B), nqb)
    h_i = jnp.arange(N_KV)[None, :, None]
    offs = jnp.arange(SLC_BLOCK)

    def one(args):
        qb, sb, pb, b = args
        blk = blocks[b]
        kg = blk[0][h_i, sb].reshape(Q_BLOCK, N_KV, n_sel * SLC_BLOCK, HEAD_DIM)
        vg = blk[1][h_i, sb].reshape(Q_BLOCK, N_KV, n_sel * SLC_BLOCK, HEAD_DIM)
        kpos = (sb[..., None] * SLC_BLOCK + offs).reshape(Q_BLOCK, N_KV, n_sel * SLC_BLOCK)
        return gathered_attend(qb, kg, vg, kpos, pb)

    out = lax.map(one, (qs, ss, ps, bs))
    return out.reshape(B, S, N_KV, GQA, HEAD_DIM)

def slc_sample(q, sel, cache_slc_kv, page_table, slc_new, pos):
    DB, DS = q.shape[:2]
    kpos = sel[..., None] * SLC_BLOCK + jnp.arange(SLC_BLOCK)
    in_past = kpos < PAST_LEN
    pp = jnp.minimum(kpos, PAST_LEN - 1)
    b_i = jnp.arange(DB)[:, None, None, None, None]
    h_i = jnp.arange(N_KV)[None, None, :, None, None]
    phys = page_table[b_i, pp // PAGE_SIZE]
    off = pp % PAGE_SIZE
    npos = jnp.clip(kpos - PAST_LEN, 0, DS - 1)

    def rows(c):
        past = cache_slc_kv[phys, off, c, h_i]
        new = slc_new[b_i, npos, c, h_i].astype(past.dtype)
        return jnp.where(in_past[..., None], past, new).reshape(DB, DS, N_KV, -1, HEAD_DIM)

    qpos = jnp.broadcast_to(pos, (DB, DS))
    return gathered_attend(q, rows(0), rows(1), kpos.reshape(DB, DS, N_KV, -1), qpos)

def win_prompt(q, win_kv, pos):
    B, S = q.shape[:2]
    nqb = S // Q_BLOCK
    span = WINDOW + Q_BLOCK
    kp = jnp.pad(win_kv, ((0, 0), (WINDOW, 0), (0, 0), (0, 0), (0, 0)))
    idx = jnp.arange(nqb)[:, None] * Q_BLOCK + jnp.arange(span)[None, :]
    kb = kp[:, idx]
    kpos = (idx - WINDOW)[:, None, :]
    qpos = pos.reshape(nqb, Q_BLOCK)[:, :, None]
    vis = (kpos >= 0) & (kpos <= qpos) & (qpos - kpos < WINDOW)
    qb = q.reshape(B, nqb, Q_BLOCK, N_KV, GQA, HEAD_DIM).astype(F32)
    s = jnp.einsum('bnqhgd,bnkhd->bnqhgk', qb, kb[:, :, :, 0].astype(F32)) * SCALE
    p = jax.nn.softmax(jnp.where(vis[None, :, :, None, None, :], s, NEG), axis=-1)
    o = jnp.einsum('bnqhgk,bnkhd->bnqhgd', p, kb[:, :, :, 1].astype(F32))
    return o.reshape(B, S, N_KV, GQA, HEAD_DIM)

def win_sample(q, keys, kpos, pos):
    s = jnp.einsum('bqhgd,bkhd->bqhgk', q.astype(F32), keys[:, :, 0].astype(F32)) * SCALE
    vis = (kpos[None, :] <= pos[:, None]) & (pos[:, None] - kpos[None, :] < WINDOW)
    p = jax.nn.softmax(jnp.where(vis[None, :, None, None, :], s, NEG), axis=-1)
    return jnp.einsum('bqhgk,bkhd->bqhgd', p, keys[:, :, 1].astype(F32))

def prompt_ctx(x, pos, g_kv, w_kv, cmp_pe, cmp_w1, cmp_w2):
    cmp_kv, slc_kv, win_kv = shared_kv(x, pos, g_kv, w_kv)
    ckv, ends = compress(pad_seq(cmp_kv, SLC_BLOCK), cmp_pe, cmp_w1, cmp_w2)
    slc_pad = pad_seq(slc_kv, SLC_BLOCK)
    n_slc = slc_pad.shape[1] // SLC_BLOCK

    def branches(q):
        o_c, p = cmp_attend(q, ckv, ends, pos)
        sel = select_blocks(p, ends, pos, n_slc)
        return o_c, slc_prompt(q, slc_pad, sel, pos), win_prompt(q, win_kv, pos)

    n_keep = min(WINDOW, x.shape[1])
    return branches, (cmp_kv, slc_kv, win_kv[:, -n_keep:])

def sample_ctx(x, pos, cache_cmp_kv, cache_slc_kv, cache_win_kv, page_table, g_kv, w_kv, cmp_pe, cmp_w1, cmp_w2):
    cmp_new, slc_new, win_new = shared_kv(x, pos, g_kv, w_kv)
    DB = x.shape[0]
    past = cache_cmp_kv[page_table].reshape(DB, -1, 2, N_KV, HEAD_DIM)
    cmp_full = pad_seq(jnp.concatenate([past, cmp_new.astype(past.dtype)], 1), SLC_BLOCK)
    ckv, ends = compress(cmp_full, cmp_pe, cmp_w1, cmp_w2)
    n_slc = cmp_full.shape[1] // SLC_BLOCK
    lb = cache_win_kv.shape[1]
    keys_w = jnp.concatenate([cache_win_kv, win_new.astype(cache_win_kv.dtype)], 1)
    kpos_w = jnp.concatenate([PAST_LEN - lb + jnp.arange(lb, dtype=jnp.int32), pos])

    def branches(q):
        o_c, p = cmp_attend(q, ckv, ends, pos)
        sel = select_blocks(p, ends, pos, n_slc)
        o_s = slc_sample(q, sel, cache_slc_kv, page_table, slc_new, pos)
        return o_c, o_s, win_sample(q, keys_w, kpos_w, pos)

    new_win = keys_w[:, -min(WINDOW, keys_w.shape[1]):]
    return branches, (cmp_new, slc_new, new_win)

def run_trunk(x, pos, pool_bufs, mem_kv, make_ctx, g_mix, w_in_a, pool_grp_w, pool_scale,
              w_in_b, b_gate, w_out, g_ffn, w_gu, w_down, g_final):
    B, S, _ = x.shape
    new_bufs = []
    branches, ctx_state = None, None
    for l in range(DEPTH):
        if l == N_A:
            branches, ctx_state = make_ctx(x)
        h = rmsnorm(x, g_mix[l])
        if l < N_A:
            u = h @ w_in_a[l]
            z, nb = causal_pool_mix(u[..., :MAIN_W], pool_bufs[l], pos, pool_grp_w[l], pool_scale[l])
            new_bufs.append(nb)
            qm = u[..., MAIN_W:]
        else:
            j = l - N_A
            u = h @ w_in_b[j]
            q = rope(u[..., :MAIN_W].reshape(B, S, N_HEADS, HEAD_DIM), pos).reshape(B, S, N_KV, GQA, HEAD_DIM)
            gates = jax.nn.sigmoid((u[..., MAIN_W:MAIN_W + GATE_W] + b_gate[j]).astype(F32))
            gates = gates.reshape(B, S, N_KV, GQA, N_BRANCH)
            o_c, o_s, o_w = branches(q)
            z = (gates[..., 0:1] * o_c + gates[..., 1:2] * o_s + gates[..., 2:3] * o_w)
            z = z.reshape(B, S, MAIN_W).astype(x.dtype)
            qm = u[..., MAIN_W + GATE_W:]
        mo = mem_attend(qm.reshape(B, S, N_MEM_HEADS, MEM_HEAD_DIM), mem_kv[l])
        x = x + jnp.concatenate([z, mo], -1) @ w_out[l]
        x = x + swiglu(rmsnorm(x, g_ffn[l]), w_gu[l], w_down[l])
    return rmsnorm(x, g_final), jnp.stack(new_bufs), ctx_state

def setup_inputs(seed: int = 0) -> dict:
    key = jax.random.key(seed)
    ks = jax.random.split(key, 32)

    def nrm(i, shape, scale):
        return jax.random.normal(ks[i], shape, F32) * scale

    def gain(i, shape):
        return 1.0 + 0.05 * jax.random.normal(ks[i], shape, F32)

    n_pages = PAST_LEN // PAGE_SIZE
    n_used = DEC_BATCH * n_pages
    n_phys = n_used + max(1, n_used // 4)
    perm = jax.random.permutation(ks[0], n_phys)
    page_table = perm[:n_used].reshape(DEC_BATCH, n_pages).astype(jnp.int32)
    win_len = min(WINDOW, PAST_LEN)
    return {
        'x_prompt': nrm(1, (BATCH, SEQ, D_MODEL), 1.0),
        'x_sample': nrm(2, (DEC_BATCH, DEC_SEQ, D_MODEL), 1.0),
        'mem_prompt': nrm(3, (BATCH, MEM_TOKENS, D_MODEL), 1.0),
        'state_pool': nrm(4, (N_A, DEC_BATCH, POOL_BUF, MAIN_W), 1.0),
        'cache_cmp_kv': nrm(5, (n_phys, PAGE_SIZE, 2, N_KV, HEAD_DIM), 1.0),
        'cache_slc_kv': nrm(6, (n_phys, PAGE_SIZE, 2, N_KV, HEAD_DIM), 1.0),
        'cache_win_kv': nrm(7, (DEC_BATCH, win_len, 2, N_KV, HEAD_DIM), 1.0),
        'cache_mem_kv': nrm(8, (DEPTH, DEC_BATCH, MEM_TOKENS, 2, N_MEM_HEADS, MEM_HEAD_DIM), 1.0),
        'page_table': page_table,
        'g_mix': gain(9, (DEPTH, D_MODEL)),
        'w_in_a': nrm(10, (N_A, D_MODEL, MAIN_W + MEM_W), D_MODEL ** -0.5),
        'pool_grp_w': nrm(11, (N_A, len(POOL_WINDOWS), POOL_GC, POOL_GC), POOL_GC ** -0.5),
        'pool_scale': gain(12, (N_A, MAIN_W)),
        'w_in_b': nrm(13, (N_B, D_MODEL, MAIN_W + GATE_W + MEM_W), D_MODEL ** -0.5),
        'b_gate': nrm(14, (N_B, GATE_W), 0.1),
        'g_kv': gain(15, (D_MODEL,)),
        'w_kv': nrm(16, (D_MODEL, N_BRANCH * 2 * N_KV * HEAD_DIM), D_MODEL ** -0.5),
        'cmp_pe': nrm(17, (2, CMP_BLOCK, HEAD_DIM), 0.1),
        'cmp_w1': nrm(18, (2, CMP_BLOCK, HEAD_DIM, CMP_HIDDEN), (CMP_BLOCK * HEAD_DIM) ** -0.5),
        'cmp_w2': nrm(19, (2, CMP_HIDDEN, HEAD_DIM), CMP_HIDDEN ** -0.5),
        'g_mem': gain(20, (DEPTH, D_MODEL)),
        'w_mem_kv': nrm(21, (DEPTH, D_MODEL, 2 * MEM_W), D_MODEL ** -0.5),
        'w_out': nrm(22, (DEPTH, MIX_W, D_MODEL), MIX_W ** -0.5),
        'g_ffn': gain(23, (DEPTH, D_MODEL)),
        'w_gu': nrm(24, (DEPTH, D_MODEL, 2 * D_FF), D_MODEL ** -0.5),
        'w_down': nrm(25, (DEPTH, D_FF, D_MODEL), D_FF ** -0.5),
        'g_final': gain(26, (D_MODEL,)),
    }

def reference(x_prompt, x_sample, mem_prompt, state_pool, cache_cmp_kv, cache_slc_kv, cache_win_kv,
              cache_mem_kv, page_table, g_mix, w_in_a, pool_grp_w, pool_scale, w_in_b, b_gate, g_kv, w_kv,
              cmp_pe, cmp_w1, cmp_w2, g_mem, w_mem_kv, w_out, g_ffn, w_gu, w_down, g_final):
    pos_p = jnp.arange(x_prompt.shape[1], dtype=jnp.int32)
    pos_s = PAST_LEN + jnp.arange(x_sample.shape[1], dtype=jnp.int32)

    mem_kv_p = jnp.stack([mem_kv_proj(mem_prompt, g_mem[l], w_mem_kv[l]) for l in range(DEPTH)])
    bufs0 = jnp.zeros((N_A, x_prompt.shape[0], POOL_BUF, MAIN_W), x_prompt.dtype)
    y_prompt, pool_p, (cmp_p, slc_p, win_p) = run_trunk(
        x_prompt, pos_p, bufs0, mem_kv_p,
        lambda h: prompt_ctx(h, pos_p, g_kv, w_kv, cmp_pe, cmp_w1, cmp_w2),
        g_mix, w_in_a, pool_grp_w, pool_scale, w_in_b, b_gate, w_out, g_ffn, w_gu, w_down, g_final)

    y_sample, pool_s, (cmp_s, slc_s, win_s) = run_trunk(
        x_sample, pos_s, state_pool, cache_mem_kv,
        lambda h: sample_ctx(h, pos_s, cache_cmp_kv, cache_slc_kv, cache_win_kv, page_table,
                             g_kv, w_kv, cmp_pe, cmp_w1, cmp_w2),
        g_mix, w_in_a, pool_grp_w, pool_scale, w_in_b, b_gate, w_out, g_ffn, w_gu, w_down, g_final)

    return (y_prompt, y_sample, pool_p, cmp_p, slc_p, win_p, mem_kv_p, pool_s, cmp_s, slc_s, win_s)


_drawn_inputs = setup_inputs


def setup_inputs(seed=0):
    import zlib

    import numpy as np

    out = dict(_drawn_inputs(seed))
    spreads = {}
    factors = {'cache_slc_kv': 2.831, 'b_gate': 8.0, 'cmp_pe': 3.136}
    for name, (base, spread) in spreads.items():
        noise = np.random.default_rng([zlib.crc32(name.encode()), seed]).standard_normal(out[name].shape)
        drawn = base * np.exp(spread * noise) if base else spread * noise
        out[name] = __import__('jax').numpy.asarray(drawn.astype(out[name].dtype))
    for name, factor in factors.items():
        out[name] = (out[name] * factor).astype(out[name].dtype)
    return out
```

```python
import concourse.bass as bass
from concourse import mybir
from contextlib import ExitStack, contextmanager
import numpy as np

D, SEQ, DB, PAST, PAGE = 2048, 256, 8, 2048, 128
T = SEQ + DB
KC = D // 128
MEM, MH, HD = 256, 4, 128
MAIN = D - MH * HD
NH, NKV = MAIN // HD, 4
G = NH // NKV
NBR = 3
GATES = NH * NBR
WIN = 512
FF = 5632
FC = FF // 128
FF_PARTS = [(0, 24), (24, 20)]
POOL_W = (2, 4, 8, 16)
PBUF = 15
PG = MAIN // 4 // 128
CS, CB, SB = 16, 32, 64
NCH = PAST // CS
NCB = NCH - 1
PCH, PCB = SEQ // CS, SEQ // CS - 1
NSB = PAST // SB
NFREE = NSB - 2
NPICK = 16 - 3
NPAGE = PAST // PAGE
HPAIR = DB * NKV
NC12, NC4 = DB * NH, DB * MH
SCALE = HD ** -0.5
EPS = 1e-6
BIG = 1e30
GELU_C = 2.0 * (2.0 / np.pi) ** 0.5
PR = 3
PCOLS = 2 * SEQ + 128

def constants():
    c = {}
    c["ident"] = np.eye(128)
    c["ones"] = np.ones((128, 128))
    pos = np.concatenate([np.arange(SEQ), np.full(DB, PAST)]).astype(np.float32)
    half = HD // 2
    inv = (np.float32(10000.0) ** (-np.arange(half, dtype=np.float32) / np.float32(half))).astype(np.float32)
    ang = (inv[:, None] * pos[None, :]).astype(np.float32).astype(np.float64)
    c["cos"] = np.concatenate([np.cos(ang), np.cos(ang)])
    c["sin"] = np.concatenate([-np.sin(ang), np.sin(ang)])
    q = np.arange(SEQ).reshape(2, 128).T
    c["causal"] = np.where(np.arange(SEQ)[None, None, :] <= q[:, :, None], 0.0, -BIG).reshape(128, -1)
    ends = np.arange(PCB) * CS + CB - 1
    vis = ends[None, None, :] <= q[:, :, None]
    c["cvis"] = np.where(vis, 0.0, -BIG).reshape(128, -1)
    c["anyvis"] = vis.any(-1).astype(np.float64)
    c["invcnt"] = np.stack([1.0 / np.minimum(np.arange(16) + 1, w) for w in POOL_W]).reshape(1, -1).repeat(128, 0)
    c["tie"] = (np.arange(NFREE)[None, :] < np.arange(NFREE)[:, None]).astype(float).reshape(1, -1).repeat(HPAIR, 0)
    st = np.arange(NCB) * CS
    j = (np.arange(NFREE) + 1) * SB
    c["cover"] = ((st[:, None] < j[None, :] + SB) & (st[:, None] + CB - 1 >= j[None, :])).astype(float)
    c["spread"] = (np.arange(NCH)[None, :] // (SB // CS) == np.arange(NSB)[:, None]).astype(float)
    own = np.where(np.arange(DB)[:, None] == np.arange(DB)[None, :], 0.0, -BIG)
    c["own"] = np.broadcast_to(own[:, :, None], (DB, DB, NH)).reshape(DB, -1)
    row = np.arange(GATES)
    c["gsel"] = np.stack([(row[:, None] == np.arange(NH)[None, :] * NBR + b) for b in range(NBR)], 1).astype(float).reshape(GATES, -1)
    off, at = {}, 0
    for k, a in c.items():
        off[k] = (at, a.shape[0], a.shape[1])
        at += a.shape[1]
    packed = np.zeros((128, at), np.float32)
    for k, a in c.items():
        packed[:a.shape[0], off[k][0]:off[k][0] + a.shape[1]] = a
    return packed, off


NS = 4
PLAN = [("x", 1, (32, 32, 32, 0))]
def _layer(l):
    ffn = []
    for p, (_, n) in enumerate(FF_PARTS):
        ffn += [(f"up{l}{p}", n // NS, (32,) * 4), (f"down{l}{p}", 4, (32,) * 4)]
    return ffn
PAIR = (16 * NPAGE, 0, 16 * NPAGE, 0)
PLAN += [("memx0", 1, (32,) * 4), ("mem0", 1, (32,) * 4), ("ua", 2, (32,) * 4), ("cmem0", 1, (64,) * 4), ("out0", 2, (32,) * 4)] + _layer(0)
PLAN += [("memx1", 1, (32,) * 4), ("mem1", 1, (32,) * 4), ("kv", 3, (32,) * 4), ("ub", 2, (32,) * 4)]
PLAN += [("cmpk", 4, PAIR), ("cmpv", 4, PAIR), ("slck", 4, PAIR), ("slcv", 4, PAIR)]
PLAN += [("wink", 1, (128,) * 4), ("winv", 1, (128,) * 4), ("cmem1", 1, (64,) * 4), ("out1", 2, (32,) * 4)] + _layer(1)
RING = {}
_r, _l = 0, [0] * NS
for _n, _it, _inc in PLAN:
    RING[_n] = (_r, tuple(_l), _it, _inc)
    _r += _it
    _l = [a + _it * b for a, b in zip(_l, _inc)]


BLOCKS = {}
_b = 0
for _n, _it, _ in PLAN:
    _b += {"down": 2, "cmpk": 2, "cmpv": 2}.get(_n[:4], 0 if _n[:4] in ("x", "memx", "cmem", "slck", "slcv", "wink", "winv") else NS) * _it
    BLOCKS[_n] = _b
STAGED_KV = 2 + 3 + 2 + 13


def at(n, name, d=0):
    k = n.get(name, 0) + d
    per = n["per"].get(name, 0)
    return n["i"] * per + k if per else k


def up(n, name, k=1):
    n[name] = n.get(name, 0) + k
    return at(n, name)


def above_zero(value):
    return not isinstance(value, int) or value > 0


@contextmanager
def rounds_of(eng, n, rounds, per):
    if rounds == 1:
        yield 0
        return
    start = dict(n)
    with eng.Fori(0, rounds) as i:
        n["i"], n["per"] = i, per
        yield i
    n["i"], n["per"] = 0, {}
    for k in per:
        assert n.get(k, 0) - start.get(k, 0) == per[k], (k, n.get(k), start.get(k), per)
        n[k] = start.get(k, 0) + rounds * per[k]


def trunk_program(nc, inp, out, coff):
    F32, I32 = mybir.dt.float32, mybir.dt.int32
    ACT, ALU, AX = mybir.ActivationFunctionType, mybir.AluOpType, mybir.AxisListType
    ds = bass.ds
    ctx = ExitStack()
    with ctx:
        def sb(name, shape, dt=F32):
            return ctx.enter_context(nc.sbuf_tensor(name, shape, dt))
        def sem(name):
            return ctx.enter_context(nc.semaphore(name))
        s_acc_free = sem("acc_free")
        s_chosen = sem("chosen")
        s_con_loaded = sem("con_loaded")
        s_diag_ready = sem("diag_ready")
        s_done = [sem(f"done{k}") for k in range(NS)]
        s_dve_step = sem("dve_step")
        s_exps = sem("exps")
        s_gate_sum = sem("gate_sum")
        s_gates = sem("gates")
        s_gates_loaded = sem("gates_loaded")
        s_gelu = sem("gelu")
        s_gelu_in = sem("gelu_in")
        s_grp_loaded = sem("grp_loaded")
        s_hT_free = sem("hT_free")
        s_h_ready = sem("h_ready")
        s_k_turned = sem("k_turned")
        s_kept = sem("kept")
        s_load = [sem(f"load{k}") for k in range(NS)]
        s_logits = sem("logits")
        s_max_ready = sem("max_ready")
        s_mean_square = sem("mean_square")
        s_memv_out = sem("memv_out")
        s_mixed = sem("mixed")
        s_p_ready = sem("p_ready")
        s_pages_loaded = sem("pages_loaded")
        s_params_loaded = sem("params_loaded")
        s_pooled = sem("pooled")
        s_psum_ready = sem("psum_ready")
        s_q_turned = sem("q_turned")
        s_root = sem("root")
        s_sc_free = sem("sc_free")
        s_sc_ready = sem("sc_ready")
        s_silu_e = sem("silu_e")
        s_squares = sem("squares")
        s_staged = sem("staged")
        s_stg_out = [sem(f"stg_out{k}") for k in range(2)]
        s_sum_ready = sem("sum_ready")
        s_tp_free = sem("tp_free")
        s_tp_ready = sem("tp_ready")
        s_state_out = sem("state_out")
        s_v_out = sem("v_out")
        s_w1_free = sem("w1_free")
        s_w1_loaded = sem("w1_loaded")
        s_win_out = [sem(f"win_out{k}") for k in range(NS)]

        ncon = sum(v[2] for v in coff.values())
        WORK = KC * T + 24 * T + 2048 + 2 * PCOLS
        con = sb("con", [128, ncon])
        ring = sb("ring", [128, NS, 4096])
        xT = sb("xT", [128, KC, T])
        hT = sb("hT", [128, KC, T])
        work = sb("work", [128, WORK])
        mkvT = sb("mkvT", [128, 8, MEM])
        memv = sb("memv", [128, 2, 512])
        stg = sb("stg", [128, 2, 512])
        kT = sb("kT", [128, 2, 512])
        gT = sb("gT", [128, 8 * KC])
        gp = sb("gp", [128, 76])
        rstd = sb("rstd", [128, T])
        wg = sb("wg", [128, KC, GATES])
        w2 = sb("w2", [128, 2, 128])
        gate = sb("gate", [GATES, T])
        bg = sb("bg", [GATES, 1])
        gN = sb("gN", [128, 2, GATES])
        cbias = sb("cbias", [128, 2])
        pages = sb("pages", [1, DB * NPAGE], I32)
        st = sb("st", [128, 4, 16])
        silu = sb("silu", [128, 3, T])
        vnew = sb("vnew", [DB, 512])
        knew = sb("knew", [128, NKV, DB])
        zacc = sb("zacc", [128, NC12])
        gb = sb("gb", [128, NBR, NC12])
        u = work[:, 0:KC * T].rearrange("p (c t) -> p c t", t=T)
        memT = work[:, 0:KC * MEM].rearrange("p (c t) -> p c t", t=MEM)
        hid = work[:, 0:24 * T].rearrange("p (c t) -> p c t", t=T)
        O0 = KC * T
        dT = work[:, O0:O0 + 12 * T].rearrange("p (c t) -> p c t", t=T)
        runs = [work[:, O0 + 12 * T + k * PG * 272:][:, 0:PG * 272].rearrange("p (c t) -> p c t", t=272) for k in range(2)]
        O1 = O0 + 12 * T + 2 * PG * 272
        stT = work[:, O1:O1 + 12 * 120].rearrange("p (c b r) -> p c b r", b=DB, r=PBUF)
        stT2 = work[:, O1:O1 + 12 * 120].rearrange("p (c n) -> p c n", n=120)
        O2 = O1 + 12 * 120
        grpw = hT[:, :, :].rearrange("p c t -> p (c t)")[:, 0:4224]
        kvT = work[:, O0:O0 + 24 * T].rearrange("p (c t) -> p c t", t=T)
        O3 = O0 + 24 * T
        vN = work[:, O3:O3 + 2048].rearrange("p (r t n) -> p r t n", r=2, t=2)
        O4 = O3 + 2048
        probs = work[:, O4:O4 + 2 * PCOLS].rearrange("p (t n) -> p t n", t=2)
        probsm = work[:, O4:O4 + 2 * PCOLS][:, 0:1024].rearrange("p (a t n) -> p a t n", a=2, t=2)
        O5 = O4 + 2 * PCOLS
        assert O5 <= WORK
        pT = sb("pT", [128, 5, SEQ])
        cbuf = sb("cbuf", [128, 240])
        cvp = sb("cvp", [128, 512])
        S = work[:, O0:O0 + 1536]
        hidS = work[:, O0 + 1536:O0 + 2044]
        tA = work[:, O0 + 2044:O0 + 2552]
        tB = work[:, O0 + 2552:O0 + 3060]
        ckT = work[:, O0 + 3060:O0 + 3572]
        cV = work[:, O0 + 3572:O0 + 4084]
        rank = work[:, O0 + 4084:O0 + 4984]
        rank2 = work[:, O0 + 4984:O0 + 5884]
        O6 = O0 + 5884
        def small(k):
            return work[:, O6 + k * 96:O6 + (k + 1) * 96]
        assert O6 + 12 * 96 <= WORK
        M1, DG, MB, Z1, RB, OO, SX, GBD = (small(k) for k in range(8))
        mrow = small(8)[:, 0:1]
        sc32, selm, selT, mask32 = (small(9)[:, 0:32], small(9)[:, 32:64], small(9)[:, 64:96], small(10)[:, 0:32])
        ps32 = small(10)[:, 32:64]
        w1 = hT[:, :, :].rearrange("p c t -> p (c t)")[:, 0:4096].rearrange("p (r f) -> p r f", f=128)
        ropet = sb("ropet", [128, 4, T])

        def C(name):
            o, r, n = coff[name]
            return con[0:r, o:o + n]
        ident, ones = C("ident"), C("ones")

        acc = ctx.enter_context(nc.psum_tensor("acc", [128, 4, 512], F32))
        tp = ctx.enter_context(nc.psum_tensor("tp", [128, 2, 512], F32))
        sc = ctx.enter_context(nc.psum_tensor("sc", [128, 2, 512], F32))

        def gcol(k):
            return gT[:, k * KC:(k + 1) * KC]
        GMIX, GKV, GMEM, GFFN, GFIN = (0, 1), 2, (3, 4), (5, 6), 7

        def ring_at(stage, i):
            return i + RING[stage][0]
        def loaded_at(stage, s, i):
            _, l, _, inc = RING[stage]
            return l[s] + inc[s] + (i * inc[s])

        def bc(ap, axis, n):
            a = ap.unsqueeze(axis)
            shape = list(a.shape)
            shape[axis] = n
            return a.to_broadcast(shape)

        block = ctx.enter_context(nc.Block())

        @block.sync
        def _(sp):
            cnt = {"i": 0, "per": {}}
            def slot_free(stage, s, i):
                before = ring_at(stage, i)
                if above_zero(before):
                    sp.wait_ge(s_done[s], before)
            sp.dma_start(con[:, :], inp["con"]).then_inc(s_con_loaded, 16)
            xs = inp["x_prompt"][0].rearrange("(t p) n -> t p n", p=128)
            sp.dma_start(ring[:, 0, 0:D], xs[0]).then_inc(s_load[0], 16)
            sp.dma_start(ring[:, 0, D:2 * D], xs[1]).then_inc(s_load[0], 16)
            sp.dma_start(ring[0:DB, 1, 0:D], inp["x_sample"].rearrange("b s n -> (b s) n")).then_inc(s_load[1], 32)
            sp.dma_start(ring[0:DB * PBUF, 2, 0:MAIN], inp["state_pool"][0].rearrange("b r n -> (b r) n")).then_inc(s_load[2], 32)
            row = 0
            for name in ("g_mix", "g_kv", "g_mem", "g_ffn", "g_final"):
                a = inp[name]
                a = a.rearrange("(c p) -> c p", p=128) if len(a.shape) == 1 else a.rearrange("l (c p) -> (l c) p", p=128)
                n = a.shape[0]
                sp.dma_start(ring[row:row + n, 3, 0:128], a).then_inc(s_params_loaded, 16)
                row += n
            sp.dma_start(ring[0:64, 3, 128:256], inp["cmp_pe"].rearrange("c r d -> (c r) d")).then_inc(s_params_loaded, 16)
            sp.dma_start(ring[64:76, 3, 128:256], inp["pool_scale"].rearrange("l (c p) -> (l c) p", p=128)).then_inc(s_params_loaded, 16)
            sp.dma_start(pages[:, :], inp["page_table"].rearrange("(a b) n -> a (b n)", a=1)).then_inc(s_pages_loaded, 16)
            sp.dma_start(bg[:, :], inp["b_gate"].rearrange("l n -> n l")).then_inc(s_gates_loaded, 16)
            sp.dma_start(wg[:, :, :], inp["w_in_b"][0, :, MAIN:MAIN + GATES].rearrange("(k p) n -> p k n", p=128)).then_inc(s_gates_loaded, 16)
            sp.dma_start(w2[:, :, :], inp["cmp_w2"].rearrange("c f d -> f c d")).then_inc(s_gates_loaded, 16)

            def load_cols(s, w, c0):
                v = ring[:, s, :].rearrange("p (k n) -> p k n", n=256)
                src = w[:, ds(c0, 256)].rearrange("(k p) n -> p k n", p=128)
                for h in range(2):
                    sp.dma_start(v[:, 8 * h:8 * h + 8, :], src[:, 8 * h:8 * h + 8, :]).then_inc(s_load[s], 16)

            def matrix(stage, w):
                with rounds_of(sp, cnt, RING[stage][2], {}) as i:
                    for s in range(NS):
                        slot_free(stage, s, i)
                        load_cols(s, w, i * (NS * 256) + s * 256)

            def mem_rows(stage):
                for s in range(NS):
                    slot_free(stage, s, 0)
                    src = inp["mem_prompt"][0, :, s * 512:(s + 1) * 512].rearrange("(t p) n -> p t n", p=128)
                    sp.dma_start(ring[:, s, 0:1024].rearrange("p (t n) -> p t n", t=2), src).then_inc(s_load[s], 32)

            def cache_mem(stage, l):
                for s in range(NS):
                    slot_free(stage, s, 0)
                    src = inp["cache_mem_kv"][l, 4 * (s % 2):4 * (s % 2) + 4, :, s // 2].rearrange("b (p t) h d -> p b t (h d)", t=2)
                    for b in range(4):
                        sp.dma_start(ring[:, s, b * 1024:(b + 1) * 1024].rearrange("p (t n) -> p t n", t=2), src[:, b]).then_inc(s_load[s], 16)

            def ffn(l):
                for p, (c0, n) in enumerate(FF_PARTS):
                    stage = f"up{l}{p}"
                    wa = inp["w_gu"][l]
                    with rounds_of(sp, cnt, RING[stage][2], {}) as i:
                        for s in range(NS):
                            slot_free(stage, s, i)
                            v = ring[:, s, :].rearrange("p (k m n) -> p k m n", m=2, n=128)
                            for m in range(2):
                                src = wa[:, ds(i * (NS * 128) + (c0 + s) * 128 + m * FF, 128)].rearrange("(k p) n -> p k n", p=128)
                                sp.dma_start(v[:, :, m, :], src).then_inc(s_load[s], 16)
                    stage = f"down{l}{p}"
                    h = n // 2
                    wd = inp["w_down"][l, c0 * 128:(c0 + n) * 128, :].rearrange("(k p) n -> p k n", p=128)
                    with rounds_of(sp, cnt, 4, {}) as i:
                        for s in range(NS):
                            slot_free(stage, s, i)
                            v = ring[:, s, 0:h * 256].rearrange("p (k n) -> p k n", n=256)
                            k0 = (s % 2) * h
                            q = h // 2
                            for a, b in ((0, q), (q, h)):
                                sp.dma_start(v[:, a:b, :], wd[:, k0 + a:k0 + b, ds(i * 512 + (s // 2) * 256, 256)]).then_inc(s_load[s], 16)

            def paged(stage, cache, c):
                with rounds_of(sp, cnt, 4, {}) as i:
                    for bb in range(2):
                        v = ring[:, 2 * bb:2 * bb + 2, :].rearrange("p s (r n) -> p (s r) n", n=512)
                        for pg in range(NPAGE):
                            page = sp.value_load(pages[0:1, ds(i * (2 * NPAGE) + bb * NPAGE + pg, 1)], min_val=0, max_val=inp[cache].shape[0] - 1)
                            if pg == 0:
                                for s in (2 * bb, 2 * bb + 1):
                                    slot_free(stage, s, i)
                            src = inp[cache][ds(page, 1), :, c].rearrange("a (n r) h d -> (a n) r (h d)", r=CS)
                            sp.dma_start(v[8 * pg:8 * pg + 8, :, :], src).then_inc(s_load[2 * bb], 16)

            def window(stage, c):
                for s in range(NS):
                    slot_free(stage, s, 0)
                    if stage == "winv":
                        sp.wait_ge(s_win_out[s], 32)
                    for b in range(2):
                        dst = ring[:, s, b * 2048:(b + 1) * 2048].rearrange("p (t n) -> p t n", t=4)
                        src = inp["cache_win_kv"][2 * s + b, 1:WIN, c].rearrange("r h d -> r (h d)")
                        for p0, p1, r in ((0, 112, 4), (112, 127, 4), (127, 128, 3)):
                            sp.dma_start(dst[p0:p1, 0:r, :], src[4 * p0:4 * p0 + r * (p1 - p0), :].rearrange("(p t) n -> p t n", t=r)).then_inc(s_load[s], 16)
                        sp.dma_start(dst[127:128, 3, :], out["win_s"][2 * s + b, WIN - 1:WIN, c].rearrange("a h d -> a (h d)")).then_inc(s_load[s], 16)

            mem_rows("memx0")
            matrix("mem0", inp["w_mem_kv"][0])
            matrix("ua", inp["w_in_a"][0])
            sp.wait_ge(s_hT_free, 1)
            gw = inp["pool_grp_w"][0].rearrange("g (k p) n -> p (g k) n", p=128)
            sp.dma_start(grpw.rearrange("p (q n) -> p q n", n=384)[:, 0:11, :], gw[:, 0:11, :]).then_inc(s_grp_loaded, 16)
            sp.dma_start(pT[:, 0:2, :].rearrange("p a b -> p (a b)")[:, 0:384], gw[:, 11, :]).then_inc(s_grp_loaded, 16)
            cache_mem("cmem0", 0)
            matrix("out0", inp["w_out"][0])
            ffn(0)
            mem_rows("memx1")
            matrix("mem1", inp["w_mem_kv"][1])
            matrix("kv", inp["w_kv"])
            for i in range(2):
                for s in range(NS):
                    slot_free("ub", s, i)
                    blk = NS * i + s
                    load_cols(s, inp["w_in_b"][0], blk * 256 + (GATES if blk >= 6 else 0))
            sp.wait_ge(s_pages_loaded, 16)
            sp.wait_ge(s_hT_free, 2)
            sp.dma_start(w1[:, :, :], inp["cmp_w1"][1].rearrange("r d f -> d r f")).then_inc(s_w1_loaded, 16)
            sp.wait_ge(s_w1_free, 1)
            sp.dma_start(w1[:, :, :], inp["cmp_w1"][0].rearrange("r d f -> d r f")).then_inc(s_w1_loaded, 16)
            paged("cmpk", "cache_cmp_kv", 0)
            sp.wait_ge(s_w1_free, 2)
            sp.dma_start(w1[:, :, :], inp["cmp_w1"][1].rearrange("r d f -> d r f")).then_inc(s_w1_loaded, 16)
            paged("cmpv", "cache_cmp_kv", 1)
            paged("slck", "cache_slc_kv", 0)
            paged("slcv", "cache_slc_kv", 1)
            for k in range(2):
                sp.wait_ge(s_stg_out[k], 32 * (STAGED_KV // 2))
            window("wink", 0)
            window("winv", 1)
            for s in range(NS):
                sp.wait_ge(s_win_out[s], 64)
            cache_mem("cmem1", 1)
            matrix("out1", inp["w_out"][1])
            ffn(1)

        @block.tensor
        def _(pe):
            cnt = {"i": 0, "per": {}}
            mmul, trans = nc.tensor.matmul, nc.tensor.transpose

            def tp_open():
                before = at(cnt, 'tp_ready', -1)
                if above_zero(before):
                    pe.wait_ge(s_tp_free, before)
                return cnt.get("tp_ready", 0) % 2
            def sc_open():
                before = at(cnt, 'sc_ready', -1)
                if above_zero(before):
                    pe.wait_ge(s_sc_free, before)
                return cnt.get("sc_ready", 0) % 2
            def tp_filled(d=0):
                before = at(cnt, 'tp_ready', -d)
                if above_zero(before):
                    pe.wait_ge(s_tp_free, before)
            def loaded(stage, s, i):
                pe.wait_ge(s_load[s], loaded_at(stage, s, i))

            def gemm(stage, rhs, n, kper=KC, parts=1):
                with rounds_of(pe, cnt, RING[stage][2], {"blocks": NS // parts}) as i:
                    for s in range(NS):
                        part = s % parts
                        loaded(stage, s, i)
                        if part == 0:
                            before = at(cnt, 'blocks', -1)
                            if above_zero(before):
                                pe.wait_ge(s_acc_free, before)
                        b = cnt.get("blocks", 0) % 2
                        w = ring[:, s, 0:kper * 256].rearrange("p (k m n) -> p k m n", m=2, n=128)
                        for m in range(2):
                            for k in range(kper):
                                mm = mmul(acc[:, 2 * b + m, 0:n], w[:, k, m, :], rhs(part * kper + k),
                                          start=(part == 0 and k == 0), stop=(part == parts - 1 and k == kper - 1))
                        mm.then_inc(s_done[s], 1)
                        if part == parts - 1:
                            cnt["blocks"] = cnt.get("blocks", 0) + 1

            def blocks_out():
                before = at(cnt, 'blocks')
                if above_zero(before):
                    pe.wait_ge(s_acc_free, before)

            def norm_sum(n):
                pe.wait_ge(s_squares, up(cnt, "squares"))
                b = sc_open()
                for k in range(KC):
                    mm = mmul(sc[:, b, 0:n], ones, hT[:, k, 0:n], start=(k == 0), stop=(k == KC - 1))
                mm.then_inc(s_sc_ready, 1)
                up(cnt, "sc_ready")

            def to_rows(src, rows):
                b = tp_open()
                for j in range(4):
                    mm = trans(tp[0:rows, b, j * 128:(j + 1) * 128], src(j), ident)
                mm.then_inc(s_tp_ready, 1)
                up(cnt, "tp_ready")

            pe.wait_ge(s_con_loaded, 16)
            pe.wait_ge(s_params_loaded, 16 * 7)
            b = tp_open()
            trans(tp[:, b, 0:128], ring[:, 3, 0:128], ident).then_inc(s_tp_ready, 1)
            up(cnt, "tp_ready")
            b = tp_open()
            trans(tp[:, b, 0:76], ring[0:76, 3, 128:256], ident[0:76, 0:76]).then_inc(s_tp_ready, 1)
            up(cnt, "tp_ready")
            loaded("x", 0, 0)
            for tt in range(2):
                for c in range(0, KC, 4):
                    b = tp_open()
                    for j in range(4):
                        mm = trans(tp[:, b, j * 128:(j + 1) * 128], ring[:, 0, tt * D + (c + j) * 128:][:, 0:128], ident)
                    mm.then_inc(s_tp_ready, 1)
                    up(cnt, "tp_ready")
            loaded("x", 1, 0)
            b = tp_open()
            for c in range(KC):
                mm = trans(tp[:, b, c * DB:(c + 1) * DB], ring[0:DB, 1, c * 128:(c + 1) * 128], ident[0:DB, 0:DB])
            mm.then_inc(s_tp_ready, 1)
            up(cnt, "tp_ready")
            loaded("x", 2, 0)
            NST = DB * PBUF
            for c in range(0, 12, 4):
                b = tp_open()
                for j in range(4):
                    mm = trans(tp[:, b, j * NST:(j + 1) * NST], ring[0:NST, 2, (c + j) * 128:][:, 0:128], ident[0:NST, 0:NST])
                mm.then_inc(s_tp_ready, 1)
                up(cnt, "tp_ready")
            for s in range(NS):
                pe.drain().then_inc(s_done[s], 1)

            def memory(l):
                for s in range(NS):
                    loaded(f"memx{l}", s, 0)
                    for tt in range(2):
                        b = tp_open()
                        for j in range(4):
                            mm = trans(tp[:, b, j * 128:(j + 1) * 128], ring[:, s, tt * 512 + j * 128:][:, 0:128], ident)
                        mm.then_inc(s_tp_ready, 1)
                        up(cnt, "tp_ready")
                    pe.drain().then_inc(s_done[s], 1)
                norm_sum(MEM)
                pe.wait_ge(s_h_ready, up(cnt, "h_ready"))
                gemm(f"mem{l}", lambda k: hT[:, k, 0:MEM], MEM)
                blocks_out()
                for tt in range(2):
                    for v in range(2):
                        to_rows(lambda j: mkvT[:, 4 * v + j, tt * 128:(tt + 1) * 128], 128)

            def prompt_memory():
                def scores(h):
                    b = sc_open()
                    for qt in range(2):
                        mm = mmul(sc[:, b, qt * MEM:(qt + 1) * MEM], u[:, NH + h, qt * 128:(qt + 1) * 128], mkvT[:, h, :], start=True, stop=True)
                    mm.then_inc(s_sc_ready, 1)
                    up(cnt, "sc_ready")
                scores(0)
                for h in range(MH):
                    if h + 1 < MH:
                        scores(h + 1)
                    pe.wait_ge(s_p_ready, up(cnt, "p_ready"))
                    b = tp_open()
                    for kt in range(2):
                        for qt in range(2):
                            mm = trans(tp[:, b, (kt * 2 + qt) * 128:][:, 0:128], probsm[:, h % 2, qt, kt * 128:(kt + 1) * 128], ident)
                    mm.then_inc(s_tp_ready, 1)
                    up(cnt, "tp_ready")
                    tp_filled()
                    b = sc_open()
                    for kt in range(2):
                        mm = mmul(sc[:, b, 0:SEQ], memv[:, kt, h * 128:(h + 1) * 128], pT[:, kt, :], start=(kt == 0), stop=(kt == 1))
                    mm.then_inc(s_sc_ready, 1)
                    up(cnt, "sc_ready")

            def turn_and_score(stage, slots, i, rhs, cols, width, done=True):
                tiles = [(s, k) for s in slots for k in range(8)]
                def turn(s, k):
                    if k == 0 and RING[stage][3][s]:
                        loaded(stage, s, i)
                    b = tp_open()
                    for h in range(NKV):
                        mm = trans(tp[:, b, h * 128:(h + 1) * 128], ring[:, s, k * 512 + h * 128:][:, 0:128], ident)
                    mm.then_inc(s_tp_ready, 1)
                    up(cnt, "tp_ready")
                turn(*tiles[0])
                bank = None
                for n, (s, k) in enumerate(tiles):
                    more = n + 1 < len(tiles)
                    if more:
                        turn(*tiles[n + 1])
                    tp_filled(1 if more else 0)
                    if n == 0:
                        bank = sc_open()
                    buf = (cnt["tp_ready"] - (2 if more else 1)) % 2
                    for h in range(NKV):
                        mm = mmul(sc[:, bank, cols(s, k) + h * width:][:, 0:width], kT[:, buf, h * 128:(h + 1) * 128], rhs(s, k, h), start=True, stop=True)
                    if k == 7 and n + 1 < len(tiles):
                        mm.then_inc(s_done[s], 1)
                mm.then_inc(s_sc_ready, 1)
                up(cnt, "sc_ready")
                pe.drain().then_inc(s_done[tiles[-1][0]], 1)

            def sample_softmax(np_, ncol, extra=False):
                pe.wait_ge(s_max_ready, up(cnt, "max_ready"))
                b = sc_open()
                mm = trans(sc[0:ncol, b, 0:np_], M1[0:np_, 0:ncol], ident[0:np_, 0:np_])
                if extra:
                    mm = trans(sc[0:ncol, b, 128:128 + DB], SX[0:DB, 0:ncol], ident[0:DB, 0:DB])
                mm.then_inc(s_sc_ready, 1)
                up(cnt, "sc_ready")
                pe.wait_ge(s_diag_ready, up(cnt, "diag_ready"))
                b = sc_open()
                mmul(sc[:, b, 0:ncol], ones[0:ncol, :], DG[0:ncol, 0:ncol], start=True, stop=True).then_inc(s_sc_ready, 1)
                up(cnt, "sc_ready")
                pe.wait_ge(s_sum_ready, up(cnt, "sum_ready"))
                b = sc_open()
                mmul(sc[:, b, 0:ncol], ones[0:np_, :], Z1[0:np_, 0:ncol], start=True, stop=True).then_inc(s_sc_ready, 1)
                up(cnt, "sc_ready")

            def sample_memory(l):
                st_ = f"cmem{l}"
                for s in range(2):
                    turn_and_score(st_, [s], 0, lambda s, k, h: u[:, NH + h, SEQ + 4 * s + k // 2:][:, 0:1],
                                   lambda s, k: k * MH, 1)
                sample_softmax(128, NC4)
                for s in range(2, 4):
                    loaded(st_, s, 0)
                b = sc_open()
                for bb in range(DB):
                    s, k = 2 + bb // 4, (bb % 4) * 2
                    for h in range(MH):
                        for tt in range(2):
                            mm = mmul(sc[:, b, bb * MH + h:][:, 0:1], ring[:, s, (k + tt) * 512 + h * 128:][:, 0:128],
                                      S[:, (bb * 2 + tt) * MH + h:][:, 0:1], start=(tt == 0), stop=(tt == 1))
                    if bb == 3:
                        mm.then_inc(s_done[2], 1)
                mm.then_inc(s_sc_ready, 1)
                up(cnt, "sc_ready")
                pe.drain().then_inc(s_done[3], 1)

            def ffn(l):
                norm_sum(T)
                pe.wait_ge(s_h_ready, up(cnt, "h_ready"))
                for p, (c0, n) in enumerate(FF_PARTS):
                    gemm(f"up{l}{p}", lambda k: hT[:, k, :], T)
                    blocks_out()
                    gemm(f"down{l}{p}", lambda k: hid[:, k, :], T, kper=n // 2, parts=2)

            memory(0)
            norm_sum(T)
            pe.wait_ge(s_h_ready, up(cnt, "h_ready"))
            gemm("ua", lambda k: hT[:, k, :], T)
            blocks_out()
            pe.drain().then_inc(s_hT_free, 1)
            for q in range(3):
                b = tp_open()
                for j in range(4):
                    mm = trans(tp[0:23, b, j * 128:(j + 1) * 128], u[:, 4 * q + j, SEQ - PBUF:T], ident)
                mm.then_inc(s_tp_ready, 1)
                up(cnt, "tp_ready")
            pe.wait_ge(s_grp_loaded, 32)
            pe.wait_ge(s_pooled, up(cnt, "pooled"))
            for g in range(4):
                for m in range(PG):
                    b = sc_open()
                    for k in range(PG):
                        q = g * PG + k
                        w = grpw[:, q * 384 + m * 128:][:, 0:128] if q < 11 else pT[:, 0:2, :].rearrange("p a b -> p (a b)")[:, m * 128:(m + 1) * 128]
                        mm = mmul(sc[:, b, 0:T], w, dT[:, g * PG + k, :], start=(k == 0), stop=(k == PG - 1))
                    mm.then_inc(s_sc_ready, 1)
                    up(cnt, "sc_ready")
            prompt_memory()
            sample_memory(0)
            pe.wait_ge(s_mixed, up(cnt, "mixed"))
            gemm("out0", lambda k: u[:, k, :], T)
            ffn(0)
            memory(1)
            norm_sum(T)
            pe.wait_ge(s_h_ready, up(cnt, "h_ready"))
            gemm("kv", lambda k: hT[:, k, :], T)
            blocks_out()
            pe.wait_ge(s_h_ready, up(cnt, "h_ready"))
            gemm("ub", lambda k: hT[:, k, :], T)
            pe.wait_ge(s_gates_loaded, 48)
            b = sc_open()
            for k in range(KC):
                mm = mmul(sc[0:GATES, b, 0:T], wg[:, k, :], hT[:, k, :], start=(k == 0), stop=(k == KC - 1))
            mm.then_inc(s_sc_ready, 1)
            up(cnt, "sc_ready")
            pe.drain().then_inc(s_hT_free, 1)
            pe.wait_ge(s_k_turned, up(cnt, "k_turned"))
            for tt in range(3):
                lo, n = (tt * 128, 128) if tt < 2 else (SEQ, DB)
                for q in range(6):
                    to_rows(lambda j: kvT[:, 4 * q + j, lo:lo + n], n)
            pe.wait_ge(s_gates, up(cnt, "gates"))
            b = tp_open()
            for qt in range(2):
                mm = trans(tp[:, b, qt * GATES:(qt + 1) * GATES], gate[:, qt * 128:(qt + 1) * 128], ident[0:GATES, 0:GATES])
            mm.then_inc(s_tp_ready, 1)
            up(cnt, "tp_ready")

            for turn_, c in enumerate((1, 0)):
                pe.wait_ge(s_w1_loaded, 16 * (turn_ + 1))
                b = sc_open()
                for r in range(CB):
                    mm = mmul(sc[:, b, 0:1], w1[:, r, :], gp[:, c * CB + r:][:, 0:1], start=(r == 0), stop=(r == CB - 1))
                mm.then_inc(s_sc_ready, 1)
                up(cnt, "sc_ready")
                b = sc_open()
                for r in range(CB):
                    src = kvT[:, c * NKV:(c + 1) * NKV, r:r + (PCB - 1) * CS + 1:CS]
                    mm = mmul(sc[:, b, 0:NKV * PCB], w1[:, r, :], src, start=(r == 0), stop=(r == CB - 1))
                mm.then_inc(s_sc_ready, 1)
                up(cnt, "sc_ready")
                if c == 1:
                    pe.drain().then_inc(s_w1_free, 1)
                pe.wait_ge(s_gelu, up(cnt, "gelu"))
                b = sc_open()
                if c == 0:
                    mm = mmul(sc[:, b, 0:NKV * PCB], w2[:, 0, :], cbuf[:, 0:NKV * PCB], start=True, stop=True)
                else:
                    for h in range(NKV):
                        mm = mmul(sc[0:PCB, b, h * 128:(h + 1) * 128], cbuf[:, h * PCB:(h + 1) * PCB], w2[:, 1, :], start=True, stop=True)
                mm.then_inc(s_sc_ready, 1)
                up(cnt, "sc_ready")
            before = at(cnt, 'sc_ready')
            if above_zero(before):
                pe.wait_ge(s_sc_free, before)

            def scores3(h):
                kv = h // G
                for br in (1, 2):
                    b = sc_open()
                    for qt in range(2):
                        mm = mmul(sc[:, b, qt * SEQ:(qt + 1) * SEQ], u[:, h, qt * 128:(qt + 1) * 128], kvT[:, br * 8 + kv, 0:SEQ], start=True, stop=True)
                    mm.then_inc(s_sc_ready, 1)
                    up(cnt, "sc_ready")
                b = sc_open()
                for qt in range(2):
                    mm = mmul(sc[:, b, qt * 16:qt * 16 + PCB], u[:, h, qt * 128:(qt + 1) * 128], cbuf[:, 60 + kv * PCB:60 + (kv + 1) * PCB], start=True, stop=True)
                mm.then_inc(s_sc_ready, 1)
                up(cnt, "sc_ready")
            pe.wait_ge(s_q_turned, up(cnt, "q_turned"))
            scores3(0)
            for h in range(NH):
                kv = h // G
                pe.wait_ge(s_p_ready, up(cnt, "p_ready"))
                for g2 in range(3):
                    b = tp_open()
                    for kt in range(2 * g2, min(2 * g2 + 2, 5)):
                        for qt in range(2):
                            mm = trans(tp[:, b, ((kt % 2) * 2 + qt) * 128:][:, 0:128], probs[:, qt, kt * 128:(kt + 1) * 128], ident)
                    mm.then_inc(s_tp_ready, 1)
                    up(cnt, "tp_ready")
                if h + 1 < NH:
                    scores3(h + 1)
                tp_filled()
                b = sc_open()
                for kt in range(5):
                    v = vN[:, kt // 2, kt % 2, kv * 128:(kv + 1) * 128] if kt < 4 else cvp[:, kv * 128:(kv + 1) * 128]
                    mm = mmul(sc[:, b, 0:SEQ], v, pT[:, kt, :], start=(kt == 0), stop=(kt == 4))
                mm.then_inc(s_sc_ready, 1)
                up(cnt, "sc_ready")

            prompt_memory()
            for br in range(NBR):
                pe.wait_ge(s_diag_ready, up(cnt, "diag_ready"))
                b = sc_open()
                mmul(sc[:, b, 0:NC12], ones[0:GATES, :], GBD[0:GATES, 0:NC12], start=True, stop=True).then_inc(s_sc_ready, 1)
                up(cnt, "sc_ready")

            def compress_rounds(stage, finish):
                with rounds_of(pe, cnt, 4, {"tp_ready": 2 * CS, "blocks": 2, "sc_ready": 4, "gelu": 2}) as i:
                    for bb in range(2):
                        tiles = [(2 * bb + r // 8, r % 8) for r in range(CS)]
                        def turn(s, k):
                            if (s, k) == tiles[0]:
                                loaded(stage, s, i)
                            b = tp_open()
                            for h in range(NKV):
                                mm = trans(tp[:, b, h * 128:(h + 1) * 128], ring[:, s, k * 512 + h * 128:][:, 0:128], ident)
                            mm.then_inc(s_tp_ready, 1)
                            up(cnt, "tp_ready")
                        turn(*tiles[0])
                        before = at(cnt, 'blocks', -1)
                        if above_zero(before):
                            pe.wait_ge(s_acc_free, before)
                        ab = cnt["blocks"] % 2
                        for r, (s, k) in enumerate(tiles):
                            more = r + 1 < CS
                            if more:
                                turn(*tiles[r + 1])
                            tp_filled(1 if more else 0)
                            buf = (cnt["tp_ready"] - (2 if more else 1)) % 2
                            kt = kT[:, buf, :].rearrange("p (h n) -> p h n", h=NKV)
                            mmul(acc[:, 2 * ab, 0:NKV * NCB], w1[:, r, :], kt[:, :, 0:NCB], start=(r == 0), stop=False)
                            mm = mmul(acc[:, 2 * ab, 0:NKV * NCB], w1[:, CS + r, :], kt[:, :, 1:NCH], start=False, stop=(r == CS - 1))
                            if r == 7:
                                mm.then_inc(s_done[s], 1)
                        mm.then_inc(s_done[2 * bb + 1], 1)
                        cnt["blocks"] += 1
                        pe.wait_ge(s_gelu, up(cnt, "gelu"))
                        finish(i, bb)

            def key_scores(i, bb):
                b = sc_open()
                mmul(sc[:, b, 0:NKV * NCB], w2[:, 0, :], hidS, start=True, stop=True).then_inc(s_sc_ready, 1)
                up(cnt, "sc_ready")
                before = at(cnt, 'sc_ready')
                if above_zero(before):
                    pe.wait_ge(s_sc_free, before)
                b = sc_open()
                for h in range(NKV):
                    q = u[:, h * G:(h + 1) * G, ds(i * 2 + (SEQ + bb), 1)].rearrange("p g b -> p (g b)")
                    mm = mmul(sc[0:NCB, b, h * G:(h + 1) * G], ckT[:, h * NCB:(h + 1) * NCB], q, start=True, stop=True)
                mm.then_inc(s_sc_ready, 1)
                up(cnt, "sc_ready")

            compress_rounds("cmpk", key_scores)
            blocks_out()
            pe.drain().then_inc(s_w1_free, 1)
            sample_softmax(NCB, NC12)
            pe.wait_ge(s_psum_ready, up(cnt, "psum_ready"))
            b = sc_open()
            mmul(sc[0:HPAIR, b, 0:NFREE], ps32[0:NCB, :], C('cover'), start=True, stop=True).then_inc(s_sc_ready, 1)
            up(cnt, "sc_ready")
            pe.wait_ge(s_chosen, up(cnt, "chosen"))
            b = sc_open()
            trans(sc[0:NSB, b, 0:HPAIR], selm[0:HPAIR, 0:NSB], ident[0:HPAIR, 0:HPAIR]).then_inc(s_sc_ready, 1)
            up(cnt, "sc_ready")
            pe.wait_ge(s_chosen, up(cnt, "chosen"))
            b = sc_open()
            mmul(sc[:, b, 0:HPAIR], C('spread'), selT[0:NSB, 0:HPAIR], start=True, stop=True).then_inc(s_sc_ready, 1)
            up(cnt, "sc_ready")

            def value_products(i, bb):
                b = sc_open()
                for h in range(NKV):
                    mm = mmul(sc[0:NCB, b, h * 128:(h + 1) * 128], hidS[:, h * NCB:(h + 1) * NCB], w2[:, 1, :], start=True, stop=True)
                mm.then_inc(s_sc_ready, 1)
                up(cnt, "sc_ready")
                before = at(cnt, 'sc_ready')
                if above_zero(before):
                    pe.wait_ge(s_sc_free, before)
                b = sc_open()
                for h in range(NKV):
                    p = S[0:NCB, ds(i * (2 * NH) + (bb * NH + h * G), G)]
                    mm = mmul(sc[:, b, h * G:(h + 1) * G], cV[0:NCB, h * 128:(h + 1) * 128], p, start=True, stop=True)
                mm.then_inc(s_sc_ready, 1)
                up(cnt, "sc_ready")

            pe.wait_ge(s_w1_loaded, 48)
            compress_rounds("cmpv", value_products)

            with rounds_of(pe, cnt, 4, {"tp_ready": 32, "sc_ready": 2}) as i:
                for bb in range(2):
                    def q3(s, k, h):
                        return u[:, h * G:(h + 1) * G, ds(i * 2 + (SEQ + bb), 1)].rearrange("p g b -> p (g b)")
                    turn_and_score("slck", [2 * bb, 2 * bb + 1], i, q3, lambda s, k: ((s % 2) * 8 + k) * NH, G)
            b = sc_open()
            for h in range(NKV):
                q = u[:, h * G:(h + 1) * G, SEQ:T].rearrange("p g b -> p b g")
                o = sc[0:DB, b, 0:NC12].rearrange("p (b c) -> p b c", c=NH)[:, :, h * G:(h + 1) * G]
                mm = mmul(o, knew[:, h, :], q, start=True, stop=True)
            mm.then_inc(s_sc_ready, 1)
            up(cnt, "sc_ready")
            sample_softmax(128, NC12, extra=True)
            with rounds_of(pe, cnt, 4, {"sc_ready": 2}) as i:
                for bb in range(2):
                    loaded("slcv", 2 * bb, i)
                    b = sc_open()
                    for h in range(NKV):
                        for r in range(CS):
                            v = ring[:, 2 * bb + r // 8, (r % 8) * 512 + h * 128:][:, 0:128]
                            p = S[:, ds(i * (2 * CS * NH) + ((bb * CS + r) * NH + h * G), G)]
                            mm = mmul(sc[:, b, h * G:(h + 1) * G], v, p, start=(r == 0), stop=(r == CS - 1))
                            if h == NKV - 1 and r == 7:
                                mm.then_inc(s_done[2 * bb], 1)
                    mm.then_inc(s_sc_ready, 1)
                    up(cnt, "sc_ready")
                    pe.drain().then_inc(s_done[2 * bb + 1], 1)
            b = sc_open()
            for h in range(NKV):
                p = SX[0:DB, 0:NC12].rearrange("p (b c) -> p b c", c=NH)[:, :, h * G:(h + 1) * G]
                o = sc[:, b, 0:NC12].rearrange("p (b c) -> p b c", c=NH)[:, :, h * G:(h + 1) * G]
                mm = mmul(o, vnew[:, h * 128:(h + 1) * 128], p, start=True, stop=True)
            mm.then_inc(s_sc_ready, 1)
            up(cnt, "sc_ready")

            for s in range(NS):
                turn_and_score("wink", [s], 0, lambda s, k, h: u[:, h * G:(h + 1) * G, SEQ + 2 * s + k // 4],
                               lambda s, k: k * NH, G)
            sample_softmax(128, NC12)
            b = sc_open()
            for bb in range(DB):
                s = bb // 2
                if bb % 2 == 0:
                    loaded("winv", s, 0)
                for h in range(NKV):
                    for tt in range(4):
                        v = ring[:, s, ((bb % 2) * 4 + tt) * 512 + h * 128:][:, 0:128]
                        p = S[:, ((bb * 4 + tt) * NH + h * G):][:, 0:G]
                        mm = mmul(sc[:, b, bb * NH + h * G:][:, 0:G], v, p, start=(tt == 0), stop=(tt == 3))
                if bb % 2 == 1 and bb < DB - 1:
                    mm.then_inc(s_done[s], 1)
            mm.then_inc(s_sc_ready, 1)
            up(cnt, "sc_ready")
            pe.drain().then_inc(s_done[3], 1)

            sample_memory(1)
            pe.wait_ge(s_mixed, up(cnt, "mixed"))
            gemm("out1", lambda k: u[:, k, :], T)
            ffn(1)
            norm_sum(T)
            pe.wait_ge(s_h_ready, up(cnt, "h_ready"))
            for tt in range(3):
                lo, n = (tt * 128, 128) if tt < 2 else (SEQ, DB)
                for q in range(4):
                    to_rows(lambda j: hT[:, 4 * q + j, lo:lo + n], n)

        @block.scalar
        def _(act):
            cnt = {"i": 0, "per": {}}

            def take(dst, src, also=None):
                act.wait_ge(s_tp_ready, up(cnt, "tp_ready"))
                b = (cnt["tp_ready"] - 1) % 2
                ins = nc.scalar.copy(dst, src(b))
                ins.then_inc(s_tp_free, 1)
                up(cnt, "tp_free")
            def to_stage(rows):
                q = cnt.get("staged", 0)
                if q >= 2:
                    act.wait_ge(s_stg_out[q % 2], 32 * (q // 2))
                take(stg[0:rows, q % 2, :], lambda b: tp[0:rows, b, :])
                act.drain().then_inc(s_staged, 1)
                up(cnt, "staged")
            def squares(src, n, stage=None):
                if stage:
                    act.wait_ge(s_acc_free, BLOCKS[stage])
                nc.scalar.activation(hT[:, :, 0:n], src, ACT.Square).then_inc(s_squares, 1)
                up(cnt, "squares")
            def root(n):
                act.wait_ge(s_mean_square, up(cnt, "mean_square"))
                nc.scalar.activation(rstd[:, 0:n], rstd[:, 0:n], ACT.Sqrt).then_inc(s_root, 1)
                up(cnt, "root")

            take(gT[:, :], lambda b: tp[:, b, 0:128])
            take(gp[:, :], lambda b: tp[:, b, 0:76])
            for tt in range(2):
                for c in range(0, KC, 4):
                    take(xT[:, c:c + 4, tt * 128:(tt + 1) * 128], lambda b: tp[:, b, :].rearrange("p (j n) -> p j n", j=4))
            take(xT[:, :, SEQ:T], lambda b: tp[:, b, 0:128].rearrange("p (c n) -> p c n", n=DB))
            for c in range(0, 12, 4):
                take(stT2[:, c:c + 4, :], lambda b: tp[:, b, 0:480].rearrange("p (j n) -> p j n", j=4))

            def memory(l):
                if l:
                    act.wait_ge(s_acc_free, BLOCKS["down01"])
                for s in range(NS):
                    for tt in range(2):
                        take(memT[:, 4 * s:4 * s + 4, tt * 128:(tt + 1) * 128], lambda b: tp[:, b, :].rearrange("p (j n) -> p j n", j=4))
                before = at(cnt, 'tp_free')
                if above_zero(before):
                    act.wait_ge(s_tp_free, before)
                squares(memT, MEM)
                root(MEM)
                if l:
                    act.wait_ge(s_memv_out, 32)
                for tt in range(2):
                    to_stage(128)
                    act.wait_ge(s_tp_ready, up(cnt, "tp_ready"))
                    ins = nc.scalar.copy(memv[:, tt, :], tp[:, (cnt["tp_ready"] - 1) % 2, :])
                    ins.then_inc(s_tp_free, 1)
                    up(cnt, "tp_free")
                    act.drain().then_inc(s_kept, 1)
                    up(cnt, "kept")
            def prompt_memory():
                def exps(h):
                    act.wait_ge(s_logits, up(cnt, "logits"))
                    nc.scalar.activation(probsm[:, h % 2], probsm[:, h % 2], ACT.Exp, scale=SCALE).then_inc(s_exps, 1)
                    up(cnt, "exps")
                exps(0)
                for h in range(MH):
                    if h + 1 < MH:
                        exps(h + 1)
                    take(pT[:, 0:2, :], lambda b: tp[:, b, :].rearrange("p (k q) -> p k q", k=2))
            def turn(n):
                for _ in range(n):
                    b = cnt["tp_ready"] % 2
                    take(kT[:, b, :], lambda b: tp[:, b, :])
            def sample_exps(np_, n, extra=False):
                act.wait_ge(s_logits, up(cnt, "logits"))
                ins = nc.scalar.activation(S[0:np_, 0:n], S[0:np_, 0:n], ACT.Exp, scale=SCALE)
                if extra:
                    ins = nc.scalar.activation(SX[0:DB, 0:NC12], SX[0:DB, 0:NC12], ACT.Exp, scale=SCALE)
                ins.then_inc(s_exps, 1)
                up(cnt, "exps")
            def sample_memory():
                turn(16)
                sample_exps(128, 2 * NC4)
            def ffn(l):
                squares(xT[:, :, :], T, f"out{l}")
                root(T)
                for p, (c0, n) in enumerate(FF_PARTS):
                    stage = f"up{l}{p}"
                    with rounds_of(act, cnt, RING[stage][2], {"silu_e": NS}) as i:
                        for s in range(NS):
                            act.wait_ge(s_done[s], ring_at(stage, i) + 1)
                            b = s % 2
                            nc.scalar.activation(silu[:, b, :], acc[:, 2 * b, 0:T], ACT.Exp, scale=-1.0).then_inc(s_silu_e, 1)
                            up(cnt, "silu_e")

            memory(0)
            squares(xT[:, :, :], T, "mem0")
            root(T)
            for q in range(3):
                to_stage(23)
            prompt_memory()
            sample_memory()
            ffn(0)
            memory(1)
            squares(xT[:, :, :], T, "mem1")
            root(T)
            for tt in range(3):
                n = 128 if tt < 2 else DB
                for q in range(6):
                    br, v = q // 2, q % 2
                    if v == 1 and br == 1 and tt == 2:
                        take(vnew[:, :], lambda b: tp[0:DB, b, :])
                        act.drain().then_inc(s_kept, 1)
                        up(cnt, "kept")
                    elif v == 1 and br >= 1 and tt < 2:
                        take(vN[:, br - 1, tt, :], lambda b: tp[:, b, :])
                        act.drain().then_inc(s_kept, 1)
                        up(cnt, "kept")
                    else:
                        to_stage(n)
            act.wait_ge(s_gate_sum, up(cnt, "gate_sum"))
            nc.scalar.activation(gate[:, :], gate[:, :], ACT.Exp, scale=-1.0).then_inc(s_exps, 1)
            up(cnt, "exps")
            take(gN[:, :, :], lambda b: tp[:, b, 0:2 * GATES].rearrange("p (t g) -> p t g", t=2))
            for c in range(2):
                act.wait_ge(s_gelu_in, up(cnt, "gelu_in"))
                nc.scalar.activation(cbuf[:, 180:240], cbuf[:, 180:240], ACT.Exp, scale=-GELU_C).then_inc(s_exps, 1)
                up(cnt, "exps")
            for h in range(NH):
                act.wait_ge(s_logits, up(cnt, "logits"))
                nc.scalar.activation(probs[:, :, 0:2 * SEQ], probs[:, :, 0:2 * SEQ], ACT.Exp, scale=SCALE)
                nc.scalar.activation(probs[:, :, 2 * SEQ:2 * SEQ + PCB], probs[:, :, 2 * SEQ:2 * SEQ + PCB], ACT.Exp, scale=SCALE).then_inc(s_exps, 1)
                up(cnt, "exps")
                for g2 in range(3):
                    n = 2 if g2 < 2 else 1
                    take(pT[:, 2 * g2:2 * g2 + n, :], lambda b: tp[:, b, 0:n * 256].rearrange("p (k q) -> p k q", k=n))
            prompt_memory()
            for c in range(2):
                with rounds_of(act, cnt, 4, {"tp_ready": 2 * CS, "tp_free": 2 * CS, "gelu_in": 2, "exps": 2}) as i:
                    for bb in range(2):
                        turn(CS)
                        act.wait_ge(s_gelu_in, up(cnt, "gelu_in"))
                        nc.scalar.activation(tB, tB, ACT.Exp, scale=-GELU_C).then_inc(s_exps, 1)
                        up(cnt, "exps")
                if c == 0:
                    sample_exps(NCB, NC12)
            with rounds_of(act, cnt, 4, {"tp_ready": 2 * CS, "tp_free": 2 * CS}) as i:
                turn(2 * CS)
            sample_exps(128, CS * NC12, extra=True)
            turn(32)
            sample_exps(128, 4 * NC12)
            sample_memory()
            ffn(1)
            squares(xT[:, :, :], T, "down11")
            root(T)
            for tt in range(3):
                for q in range(4):
                    to_stage(128 if tt < 2 else DB)

        @block.gpsimd
        def _(pool):
            cnt = {"i": 0, "per": {}}
            staged = [0]
            def from_stage(rows, *dsts):
                q = staged[0]
                staged[0] += 1
                pool.wait_ge(s_staged, up(cnt, "staged"))
                for r0, r1, dst in dsts:
                    pool.dma_start(dst, stg[r0:r1, q % 2, :]).then_inc(s_stg_out[q % 2], 32 // len(dsts))
                    up(cnt, f"stg_out{q % 2}", 32 // len(dsts))
            pool.dma_start(out["pool_s"][0, :, 0:PBUF - 1, :], inp["state_pool"][0, :, 1:PBUF, :]).then_inc(s_state_out, 16)
            up(cnt, "state_out", 16)
            def memory(l):
                for tt in range(2):
                    rows = out["mem"][l, 0, tt * 128:(tt + 1) * 128]
                    from_stage(128, (0, 128, rows[:, 0].rearrange("r h d -> r (h d)")))
                    pool.wait_ge(s_kept, up(cnt, "kept"))
                    pool.dma_start(rows[:, 1].rearrange("r h d -> r (h d)"), memv[:, tt, :]).then_inc(s_memv_out, 16)
                    up(cnt, "memv_out", 16)
            memory(0)
            for q in range(3):
                cols = slice(q * 512, (q + 1) * 512)
                from_stage(23, (0, PBUF, out["pool_p"][0, 0, :, cols]), (PBUF, 23, out["pool_s"][0, :, PBUF - 1, cols]))
            memory(1)
            for tt in range(3):
                for q in range(6):
                    br, v = q // 2, q % 2
                    o = (out["cmp_p"], out["slc_p"], out["win_p"])[br] if tt < 2 else (out["cmp_s"], out["slc_s"], out["win_s"])[br]
                    if tt < 2:
                        dst = o[0, tt * 128:(tt + 1) * 128, v].rearrange("r h d -> r (h d)")
                    elif br < 2:
                        dst = o[:, 0, v].rearrange("b h d -> b (h d)")
                    else:
                        dst = o[:, WIN - 1, v].rearrange("b h d -> b (h d)")
                    if v == 1 and br == 1 and tt == 2:
                        pool.wait_ge(s_kept, up(cnt, "kept"))
                        pool.dma_start(dst, vnew[:, :]).then_inc(s_v_out, 16)
                        up(cnt, "v_out", 16)
                    elif v == 1 and br >= 1 and tt < 2:
                        pool.wait_ge(s_kept, up(cnt, "kept"))
                        pool.dma_start(dst, vN[:, br - 1, tt, :]).then_inc(s_v_out, 16)
                        up(cnt, "v_out", 16)
                    else:
                        from_stage(128 if tt < 2 else DB, (0, 128 if tt < 2 else DB, dst))
            for c, stage in enumerate(("wink", "winv")):
                for s in range(NS):
                    pool.wait_ge(s_load[s], loaded_at(stage, s, 0))
                    for b in range(2):
                        src = ring[:, s, b * 2048:(b + 1) * 2048].rearrange("p (t n) -> p t n", t=4)
                        dst = out["win_s"][2 * s + b, :, c].rearrange("(p t) h d -> p t (h d)", t=4)
                        pool.dma_start(dst, src).then_inc(s_win_out[s], 16)
                        up(cnt, f"win_out{s}", 16)
            for tt in range(3):
                for q in range(4):
                    n = 128 if tt < 2 else DB
                    cols = slice(q * 512, (q + 1) * 512)
                    dst = out["y_p"][0, tt * 128:(tt + 1) * 128, cols] if tt < 2 else out["y_s"][:, 0, cols]
                    from_stage(n, (0, n, dst))
            for k in range(2):
                pool.wait_ge(s_stg_out[k], at(cnt, f"stg_out{k}"))
            for s in range(NS):
                pool.wait_ge(s_win_out[s], at(cnt, f"win_out{s}"))
            pool.wait_ge(s_state_out, at(cnt, "state_out"))
            pool.wait_ge(s_memv_out, at(cnt, "memv_out"))
            pool.wait_ge(s_v_out, at(cnt, "v_out"))

        @block.vector
        def _(dve):
            cnt = {"i": 0, "per": {}}
            v = nc.vector
            def sc_take():
                dve.wait_ge(s_sc_ready, up(cnt, "sc_ready"))
                return (cnt["sc_ready"] - 1) % 2

            def scaled(src, n, k):
                v.tensor_tensor(hT[:, :, 0:n], src, bc(rstd[:, 0:n], 1, KC), ALU.mult).then_inc(s_dve_step, 1)
                dve.wait_ge(s_dve_step, up(cnt, "dve_step"))
                v.tensor_tensor(hT[:, :, 0:n], hT[:, :, 0:n], bc(gcol(k), 2, n), ALU.mult).then_inc(s_h_ready, 1)
                dve.wait_ge(s_h_ready, up(cnt, "h_ready"))
            def norm(src, n, k):
                b = sc_take()
                v.tensor_scalar(rstd[:, 0:n], sc[:, b, 0:n], 1.0 / KC / 128, EPS, ALU.mult, ALU.add).then_inc(s_sc_free, 1)
                dve.wait_ge(s_sc_free, up(cnt, "sc_free"))
                dve.drain().then_inc(s_mean_square, 1)
                up(cnt, "mean_square")
                dve.wait_ge(s_root, up(cnt, "root"))
                v.reciprocal(rstd[:, 0:n], rstd[:, 0:n]).then_inc(s_dve_step, 1)
                dve.wait_ge(s_dve_step, up(cnt, "dve_step"))
                scaled(src, n, k)

            def blocks(stage, per, fn, steps=0, more=None):
                with rounds_of(dve, cnt, RING[stage][2], {"acc_free": NS // per, "dve_step": steps, **(more or {})}) as i:
                    for s in range(per - 1, NS, per):
                        dve.wait_ge(s_done[s], ring_at(stage, i) + 1)
                        fn(i, s, 2 * ((s // per) % 2))
            def keep(dst, n):
                def taken(i, s, b):
                    v.tensor_scalar(dst[:, ds(i * (2 * NS) + 2 * s, 2), 0:n], acc[:, b:b + 2, 0:n], 1.0, None, ALU.mult).then_inc(s_acc_free, 1)
                    dve.wait_ge(s_acc_free, up(cnt, "acc_free"))
                return taken

            def memory(l):
                norm(memT, MEM, GMEM[l])
                def taken(i, s, b):
                    v.tensor_scalar(mkvT[:, 2 * s:2 * s + 2, :], acc[:, b:b + 2, 0:MEM], 1.0, None, ALU.mult).then_inc(s_acc_free, 1)
                    dve.wait_ge(s_acc_free, up(cnt, "acc_free"))
                blocks(f"mem{l}", 1, taken)

            def prompt_memory():
                def shift(h):
                    b = sc_take()
                    x = sc[:, b, :].rearrange("p (t n) -> p t n", t=2)
                    v.tensor_reduce(st[:, 0, 0:2], x, AX.X, ALU.max).then_inc(s_dve_step, 1)
                    dve.wait_ge(s_dve_step, up(cnt, "dve_step"))
                    v.tensor_tensor(probsm[:, h % 2], x, bc(st[:, 0, 0:2], 2, MEM), ALU.subtract).then_inc(s_sc_free, 1)
                    dve.wait_ge(s_sc_free, up(cnt, "sc_free"))
                    dve.drain().then_inc(s_logits, 1)
                    up(cnt, "logits")
                shift(0)
                for h in range(MH):
                    dve.wait_ge(s_exps, up(cnt, "exps"))
                    v.tensor_reduce(st[:, 1, 0:2], probsm[:, h % 2], AX.X, ALU.add).then_inc(s_dve_step, 1)
                    dve.wait_ge(s_dve_step, up(cnt, "dve_step"))
                    v.reciprocal(st[:, 2, 0:2], st[:, 1, 0:2]).then_inc(s_dve_step, 1)
                    dve.wait_ge(s_dve_step, up(cnt, "dve_step"))
                    v.tensor_tensor(probsm[:, h % 2], probsm[:, h % 2], bc(st[:, 2, 0:2], 2, MEM), ALU.mult).then_inc(s_p_ready, 1)
                    dve.wait_ge(s_p_ready, up(cnt, "p_ready"))
                    if h + 1 < MH:
                        shift(h + 1)
                    b = sc_take()
                    v.tensor_scalar(u[:, NH + h, 0:SEQ], sc[:, b, 0:SEQ], 1.0, None, ALU.mult).then_inc(s_sc_free, 1)
                    dve.wait_ge(s_sc_free, up(cnt, "sc_free"))

            def sample_softmax(np_, tn, c, extra=False):
                n = DB * c
                x = S[0:np_, 0:tn * n].rearrange("p (b t c) -> p b t c", b=DB, t=tn)
                def cols(a, np2):
                    return a[0:np2, 0:n].rearrange("p (b c) -> p b c", b=DB)
                v.tensor_reduce(cols(M1, np_), x.rearrange('p b t c -> p b c t'), AX.X, ALU.max).then_inc(s_max_ready, 1)
                dve.wait_ge(s_max_ready, up(cnt, "max_ready"))
                b = sc_take()
                v.tensor_reduce(mrow[0:n, :], sc[0:n, b, 0:128 + DB if extra else np_], AX.X, ALU.max).then_inc(s_sc_free, 1)
                dve.wait_ge(s_sc_free, up(cnt, "sc_free"))
                v.tensor_scalar(DG[0:n, 0:n], ident[0:n, 0:n], mrow[0:n, :], None, ALU.mult).then_inc(s_diag_ready, 1)
                dve.wait_ge(s_diag_ready, up(cnt, "diag_ready"))
                b = sc_take()
                v.tensor_scalar(MB[:, 0:n], sc[:, b, 0:n], 1.0, None, ALU.mult).then_inc(s_sc_free, 1)
                dve.wait_ge(s_sc_free, up(cnt, "sc_free"))
                if extra:
                    v.tensor_tensor(SX[0:DB, 0:n], SX[0:DB, 0:n], MB[0:DB, 0:n], ALU.subtract).then_inc(s_dve_step, 1)
                    dve.wait_ge(s_dve_step, up(cnt, "dve_step"))
                v.tensor_tensor(x, x, bc(cols(MB, np_), 2, tn), ALU.subtract).then_inc(s_logits, 1)
                dve.wait_ge(s_logits, up(cnt, "logits"))
                dve.wait_ge(s_exps, up(cnt, "exps"))
                z = v.tensor_reduce(cols(Z1, np_), x.rearrange('p b t c -> p b c t'), AX.X, ALU.add)
                if not extra:
                    z.then_inc(s_sum_ready, 1)
                    up(cnt, 'sum_ready')
                if extra:
                    z.then_inc(s_dve_step, 1)
                    dve.wait_ge(s_dve_step, up(cnt, 'dve_step'))
                    v.tensor_tensor(Z1[0:DB, 0:n], Z1[0:DB, 0:n], SX[0:DB, 0:n], ALU.add).then_inc(s_sum_ready, 1)
                    dve.wait_ge(s_sum_ready, up(cnt, "sum_ready"))
                b = sc_take()
                v.reciprocal(RB[:, 0:n], sc[:, b, 0:n]).then_inc(s_sc_free, 1)
                dve.wait_ge(s_sc_free, up(cnt, "sc_free"))

            def sample_memory():
                for s in range(2):
                    b = sc_take()
                    v.tensor_scalar(S[:, s * 32:(s + 1) * 32], sc[:, b, 0:32], 1.0, None, ALU.mult).then_inc(s_sc_free, 1)
                    dve.wait_ge(s_sc_free, up(cnt, "sc_free"))
                sample_softmax(128, 2, MH)
                b = sc_take()
                v.tensor_tensor(u[:, NH:KC, SEQ:T].rearrange('p h b -> p b h'), sc[:, b, 0:NC4].rearrange('p (b h) -> p b h', b=DB), RB[:, 0:NC4].rearrange('p (b h) -> p b h', b=DB), ALU.mult).then_inc(s_sc_free, 1)
                dve.wait_ge(s_sc_free, up(cnt, "sc_free"))

            def residual(stage, per):
                def added(i, s, b):
                    x = xT[:, ds(i * (2 * NS // per) + 2 * (s // per), 2), :]
                    v.tensor_tensor(x, acc[:, b:b + 2, 0:T], x, ALU.add).then_inc(s_acc_free, 1)
                    dve.wait_ge(s_acc_free, up(cnt, "acc_free"))
                blocks(stage, per, added)
            def ffn(l):
                norm(xT[:, :, :], T, GFFN[l])
                for p, (c0, n) in enumerate(FF_PARTS):
                    def hidden(i, s, b):
                        dve.wait_ge(s_silu_e, up(cnt, "silu_e"))
                        e = silu[:, s % 2, :]
                        v.tensor_scalar(e, e, 1.0, None, ALU.add).then_inc(s_dve_step, 1)
                        dve.wait_ge(s_dve_step, up(cnt, "dve_step"))
                        v.reciprocal(e, e).then_inc(s_dve_step, 1)
                        dve.wait_ge(s_dve_step, up(cnt, "dve_step"))
                        v.tensor_tensor(e, acc[:, b, 0:T], e, ALU.mult).then_inc(s_dve_step, 1)
                        dve.wait_ge(s_dve_step, up(cnt, "dve_step"))
                        v.tensor_tensor(hid[:, ds(i * NS + s, 1), :].rearrange('p a t -> p (a t)'), acc[:, b + 1, 0:T], e, ALU.mult).then_inc(s_acc_free, 1)
                        dve.wait_ge(s_acc_free, up(cnt, "acc_free"))
                    blocks(f"up{l}{p}", 1, hidden, 3 * NS, {"silu_e": NS})
                    residual(f"down{l}{p}", 2)

            def rotate(x):
                v.tensor_scalar(ropet[0:64], x[64:128], 1.0, None, ALU.mult).then_inc(s_dve_step, 1)
                dve.wait_ge(s_dve_step, up(cnt, "dve_step"))
                v.tensor_scalar(ropet[64:128], x[0:64], 1.0, None, ALU.mult).then_inc(s_dve_step, 1)
                dve.wait_ge(s_dve_step, up(cnt, "dve_step"))
                v.tensor_tensor(x, x, bc(C('cos'), 1, 4), ALU.mult).then_inc(s_dve_step, 1)
                dve.wait_ge(s_dve_step, up(cnt, "dve_step"))
                v.tensor_tensor(ropet[:, :, :], ropet[:, :, :], bc(C('sin'), 1, 4), ALU.mult).then_inc(s_dve_step, 1)
                dve.wait_ge(s_dve_step, up(cnt, "dve_step"))
                v.tensor_tensor(x, x, ropet[:, :, :], ALU.add).then_inc(s_dve_step, 1)
                dve.wait_ge(s_dve_step, up(cnt, "dve_step"))

            def gelu(src, dst, x, w, bias, freed):
                v.tensor_scalar(x, src, bias, None, ALU.add).then_inc((s_sc_free if freed == 'sc_free' else s_acc_free), 1)
                dve.wait_ge((s_sc_free if freed == 'sc_free' else s_acc_free), up(cnt, freed))
                v.tensor_tensor(w, x, x, ALU.mult).then_inc(s_dve_step, 1)
                dve.wait_ge(s_dve_step, up(cnt, "dve_step"))
                v.tensor_scalar(w, w, 0.044715, 1.0, ALU.mult, ALU.add).then_inc(s_dve_step, 1)
                dve.wait_ge(s_dve_step, up(cnt, "dve_step"))
                v.tensor_tensor(w, w, x, ALU.mult).then_inc(s_gelu_in, 1)
                dve.wait_ge(s_gelu_in, up(cnt, "gelu_in"))
                dve.wait_ge(s_exps, up(cnt, "exps"))
                v.tensor_scalar(w, w, 1.0, None, ALU.add).then_inc(s_dve_step, 1)
                dve.wait_ge(s_dve_step, up(cnt, "dve_step"))
                v.reciprocal(w, w).then_inc(s_dve_step, 1)
                dve.wait_ge(s_dve_step, up(cnt, "dve_step"))
                v.tensor_tensor(dst, x, w, ALU.mult).then_inc(s_gelu, 1)
                dve.wait_ge(s_gelu, up(cnt, "gelu"))

            memory(0)
            norm(xT[:, :, :], T, GMIX[0])
            v.memset(runs[0][:, :, 0:16], 0.0).then_inc(s_dve_step, 1)
            dve.wait_ge(s_dve_step, up(cnt, "dve_step"))
            v.memset(runs[1][:, :, 0:16], 0.0).then_inc(s_dve_step, 1)
            dve.wait_ge(s_dve_step, up(cnt, "dve_step"))
            blocks("ua", 1, keep(u, T))
            for g, w in enumerate(POOL_W):
                x = u[:, PG * g:PG * (g + 1), 0:SEQ]
                d = dT[:, PG * g:PG * (g + 1), :]
                cur = 0
                v.tensor_scalar(runs[0][:, :, 16:], x, 1.0, None, ALU.mult).then_inc(s_dve_step, 1)
                dve.wait_ge(s_dve_step, up(cnt, "dve_step"))
                for k in range(g + 1):
                    v.tensor_tensor(runs[1 - cur][:, :, 16:], runs[cur][:, :, 16:], runs[cur][:, :, 16 - 2 ** k:272 - 2 ** k], ALU.add).then_inc(s_dve_step, 1)
                    dve.wait_ge(s_dve_step, up(cnt, "dve_step"))
                    cur = 1 - cur
                v.tensor_scalar(d[:, :, 0:SEQ], runs[cur][:, :, 16:], 1.0 / w, None, ALU.mult).then_inc(s_dve_step, 1)
                dve.wait_ge(s_dve_step, up(cnt, "dve_step"))
                invc = C("invcnt")[:, g * 16:(g + 1) * 16]
                v.tensor_tensor(d[:, :, 0:16], runs[cur][:, :, 16:32], bc(invc, 1, PG), ALU.mult).then_inc(s_dve_step, 1)
                dve.wait_ge(s_dve_step, up(cnt, "dve_step"))
                v.tensor_tensor(d[:, :, 0:SEQ], d[:, :, 0:SEQ], x, ALU.subtract).then_inc(s_dve_step, 1)
                dve.wait_ge(s_dve_step, up(cnt, "dve_step"))
                new = u[:, PG * g:PG * (g + 1), SEQ:T]
                v.tensor_reduce(d[:, :, SEQ:T], stT[:, PG * g:PG * (g + 1), :, PBUF - (w - 1):PBUF], AX.X, ALU.add).then_inc(s_dve_step, 1)
                dve.wait_ge(s_dve_step, up(cnt, "dve_step"))
                v.tensor_tensor(d[:, :, SEQ:T], d[:, :, SEQ:T], new, ALU.add).then_inc(s_dve_step, 1)
                dve.wait_ge(s_dve_step, up(cnt, "dve_step"))
                v.tensor_scalar(d[:, :, SEQ:T], d[:, :, SEQ:T], 1.0 / w, None, ALU.mult).then_inc(s_dve_step, 1)
                dve.wait_ge(s_dve_step, up(cnt, "dve_step"))
                v.tensor_tensor(d[:, :, SEQ:T], d[:, :, SEQ:T], new, ALU.subtract).then_inc(s_dve_step, 1)
                dve.wait_ge(s_dve_step, up(cnt, "dve_step"))
            dve.drain().then_inc(s_pooled, 1)
            up(cnt, "pooled")
            for c in range(4 * PG):
                b = sc_take()
                v.tensor_scalar(u[:, c, :], sc[:, b, 0:T], gp[:, 64 + c:65 + c], None, ALU.mult).then_inc(s_sc_free, 1)
                dve.wait_ge(s_sc_free, up(cnt, "sc_free"))
            prompt_memory()
            sample_memory()
            dve.drain().then_inc(s_mixed, 1)
            up(cnt, "mixed")
            residual("out0", 1)
            ffn(0)

            memory(1)
            norm(xT[:, :, :], T, GKV)
            blocks("kv", 1, keep(kvT, T))
            scaled(xT[:, :, :], T, GMIX[1])
            for br in range(NBR):
                rotate(kvT[:, br * 8:br * 8 + 4, :])
            v.tensor_scalar(knew[:, :, :], kvT[:, 8:12, SEQ:T], 1.0, None, ALU.mult).then_inc(s_dve_step, 1)
            dve.wait_ge(s_dve_step, up(cnt, "dve_step"))
            dve.drain().then_inc(s_k_turned, 1)
            up(cnt, "k_turned")
            blocks("ub", 1, keep(u, T))
            b = sc_take()
            v.tensor_scalar(gate[:, :], sc[0:GATES, b, 0:T], bg[:, 0:1], None, ALU.add).then_inc(s_sc_free, 1)
            dve.wait_ge(s_sc_free, up(cnt, "sc_free"))
            dve.drain().then_inc(s_gate_sum, 1)
            up(cnt, "gate_sum")
            dve.wait_ge(s_exps, up(cnt, "exps"))
            v.tensor_scalar(gate[:, :], gate[:, :], 1.0, None, ALU.add).then_inc(s_dve_step, 1)
            dve.wait_ge(s_dve_step, up(cnt, "dve_step"))
            v.reciprocal(gate[:, :], gate[:, :]).then_inc(s_gates, 1)
            dve.wait_ge(s_gates, up(cnt, "gates"))
            for q in range(3):
                rotate(u[:, 4 * q:4 * q + 4, :])
            v.memset(cvp[:, :], 0.0).then_inc(s_dve_step, 1)
            dve.wait_ge(s_dve_step, up(cnt, "dve_step"))
            v.memset(probs[:, :, 2 * SEQ:PCOLS], 0.0).then_inc(s_dve_step, 1)
            dve.wait_ge(s_dve_step, up(cnt, "dve_step"))
            dve.drain().then_inc(s_q_turned, 1)
            up(cnt, "q_turned")
            n = NKV * PCB
            for c in (1, 0):
                b = sc_take()
                v.tensor_scalar(cbias[:, c:c + 1], sc[:, b, 0:1], 1.0, None, ALU.mult).then_inc(s_sc_free, 1)
                dve.wait_ge(s_sc_free, up(cnt, "sc_free"))
                b = sc_take()
                gelu(sc[:, b, 0:n], cbuf[:, 0:n], cbuf[:, 120:180], cbuf[:, 180:240], cbias[:, c:c + 1], "sc_free")
                b = sc_take()
                if c == 0:
                    v.tensor_scalar(cbuf[:, 60:120], sc[:, b, 0:n], 1.0, None, ALU.mult).then_inc(s_sc_free, 1)
                    dve.wait_ge(s_sc_free, up(cnt, "sc_free"))
                else:
                    v.tensor_scalar(cvp[0:PCB, :], sc[0:PCB, b, :], 1.0, None, ALU.mult).then_inc(s_sc_free, 1)
                    dve.wait_ge(s_sc_free, up(cnt, "sc_free"))

            both = probs[:, :, 0:2 * SEQ].rearrange("p t (r n) -> p t r n", r=2)
            cmp = probs[:, :, 2 * SEQ:2 * SEQ + PCB]
            def six(k):
                return st[:, k, 0:6].rearrange("p (t r) -> p t r", t=2)
            def shift3(h):
                causal = C("causal").rearrange("p (t n) -> p t n", t=2)
                for r in range(2):
                    b = sc_take()
                    v.tensor_tensor(both[:, :, r, :], sc[:, b, :].rearrange('p (t n) -> p t n', t=2), causal, ALU.add).then_inc(s_sc_free, 1)
                    dve.wait_ge(s_sc_free, up(cnt, "sc_free"))
                b = sc_take()
                v.tensor_tensor(cmp, sc[:, b, 0:32].rearrange('p (t n) -> p t n', t=2)[:, :, 0:PCB], C('cvis').rearrange('p (t n) -> p t n', t=2), ALU.add).then_inc(s_sc_free, 1)
                dve.wait_ge(s_sc_free, up(cnt, "sc_free"))
                v.tensor_reduce(six(0)[:, :, 0:2], both, AX.X, ALU.max).then_inc(s_dve_step, 1)
                dve.wait_ge(s_dve_step, up(cnt, "dve_step"))
                v.tensor_reduce(six(0)[:, :, 2:3], cmp, AX.X, ALU.max).then_inc(s_dve_step, 1)
                dve.wait_ge(s_dve_step, up(cnt, "dve_step"))
                v.tensor_tensor(both, both, bc(six(0)[:, :, 0:2], 3, SEQ), ALU.subtract).then_inc(s_dve_step, 1)
                dve.wait_ge(s_dve_step, up(cnt, "dve_step"))
                v.tensor_tensor(cmp, cmp, six(0)[:, :, 2:3].to_broadcast([128, 2, PCB]), ALU.subtract).then_inc(s_logits, 1)
                dve.wait_ge(s_logits, up(cnt, "logits"))
            shift3(0)
            for h in range(NH):
                dve.wait_ge(s_exps, up(cnt, "exps"))
                v.tensor_reduce(six(1)[:, :, 0:2], both, AX.X, ALU.add).then_inc(s_dve_step, 1)
                dve.wait_ge(s_dve_step, up(cnt, "dve_step"))
                v.tensor_reduce(six(1)[:, :, 2:3], cmp, AX.X, ALU.add).then_inc(s_dve_step, 1)
                dve.wait_ge(s_dve_step, up(cnt, "dve_step"))
                v.reciprocal(st[:, 2, 0:6], st[:, 1, 0:6]).then_inc(s_dve_step, 1)
                dve.wait_ge(s_dve_step, up(cnt, "dve_step"))
                v.tensor_tensor(six(2)[:, :, 0:2], six(2)[:, :, 0:2], gN[:, :, NBR * h + 1:NBR * h + 3], ALU.mult).then_inc(s_dve_step, 1)
                dve.wait_ge(s_dve_step, up(cnt, "dve_step"))
                v.tensor_tensor(six(2)[:, :, 2:3], six(2)[:, :, 2:3], gN[:, :, NBR * h:NBR * h + 1], ALU.mult).then_inc(s_dve_step, 1)
                dve.wait_ge(s_dve_step, up(cnt, "dve_step"))
                v.tensor_tensor(six(2)[:, :, 2:3], six(2)[:, :, 2:3], C('anyvis').unsqueeze(2), ALU.mult).then_inc(s_dve_step, 1)
                dve.wait_ge(s_dve_step, up(cnt, "dve_step"))
                v.tensor_tensor(both, both, bc(six(2)[:, :, 0:2], 3, SEQ), ALU.mult).then_inc(s_dve_step, 1)
                dve.wait_ge(s_dve_step, up(cnt, "dve_step"))
                v.tensor_tensor(cmp, cmp, six(2)[:, :, 2:3].to_broadcast([128, 2, PCB]), ALU.mult).then_inc(s_p_ready, 1)
                dve.wait_ge(s_p_ready, up(cnt, "p_ready"))
                if h + 1 < NH:
                    shift3(h + 1)
                b = sc_take()
                v.tensor_scalar(u[:, h, 0:SEQ], sc[:, b, 0:SEQ], 1.0, None, ALU.mult).then_inc(s_sc_free, 1)
                dve.wait_ge(s_sc_free, up(cnt, "sc_free"))
            prompt_memory()
            for br in range(NBR):
                g3 = GBD[0:GATES, :].rearrange("p (b c) -> p b c", b=DB)
                sel = C("gsel")[:, br * NH:(br + 1) * NH]
                v.tensor_tensor(g3, bc(sel, 1, DB), bc(gate[:, SEQ:T], 2, NH), ALU.mult).then_inc(s_diag_ready, 1)
                dve.wait_ge(s_diag_ready, up(cnt, "diag_ready"))
                b = sc_take()
                v.tensor_scalar(gb[:, br, :], sc[:, b, 0:NC12], 1.0, None, ALU.mult).then_inc(s_sc_free, 1)
                dve.wait_ge(s_sc_free, up(cnt, "sc_free"))

            def add_branch(br):
                v.tensor_tensor(OO, OO, RB, ALU.mult).then_inc(s_dve_step, 1)
                dve.wait_ge(s_dve_step, up(cnt, "dve_step"))
                v.tensor_tensor(OO, OO, gb[:, br, :], ALU.mult).then_inc(s_dve_step, 1)
                dve.wait_ge(s_dve_step, up(cnt, "dve_step"))
                if br == 0:
                    v.tensor_scalar(zacc[:, :], OO, 1.0, None, ALU.mult).then_inc(s_dve_step, 1)
                    dve.wait_ge(s_dve_step, up(cnt, "dve_step"))
                else:
                    v.tensor_tensor(zacc[:, :], zacc[:, :], OO, ALU.add).then_inc(s_dve_step, 1)
                    dve.wait_ge(s_dve_step, up(cnt, "dve_step"))
            nn = NKV * NCB
            def key_block(i, s, b):
                gelu(acc[:, b, 0:nn], hidS, tA[:, 0:nn], tB[:, 0:nn], cbias[:, 0:1], "acc_free")
                b = sc_take()
                v.tensor_scalar(ckT[:, 0:nn], sc[:, b, 0:nn], 1.0, None, ALU.mult).then_inc(s_sc_free, 1)
                dve.wait_ge(s_sc_free, up(cnt, "sc_free"))
                b = sc_take()
                v.tensor_scalar(S[0:NCB, ds(i * (2 * NH) + s // 2 * NH, NH)], sc[0:NCB, b, 0:NH], 1.0, None, ALU.mult).then_inc(s_sc_free, 1)
                dve.wait_ge(s_sc_free, up(cnt, "sc_free"))
            def value_block(i, s, b):
                gelu(acc[:, b, 0:nn], hidS, tA[:, 0:nn], tB[:, 0:nn], cbias[:, 1:2], "acc_free")
                b = sc_take()
                v.tensor_scalar(cV[0:NCB, :], sc[0:NCB, b, :], 1.0, None, ALU.mult).then_inc(s_sc_free, 1)
                dve.wait_ge(s_sc_free, up(cnt, "sc_free"))
                b = sc_take()
                v.tensor_scalar(OO[:, ds(i * (2 * NH) + s // 2 * NH, NH)], sc[:, b, 0:NH], 1.0, None, ALU.mult).then_inc(s_sc_free, 1)
                dve.wait_ge(s_sc_free, up(cnt, "sc_free"))
            per = {"sc_ready": 4, "sc_free": 4, "gelu": 2, "gelu_in": 2, "exps": 2}
            blocks("cmpk", 2, key_block, 8, per)
            sample_softmax(NCB, 1, NH)
            v.tensor_tensor(MB[0:NCB, :], S[0:NCB, 0:NC12], RB[0:NCB, :], ALU.mult).then_inc(s_dve_step, 1)
            dve.wait_ge(s_dve_step, up(cnt, "dve_step"))
            v.tensor_reduce(ps32[0:NCB, :], MB[0:NCB, :].rearrange('p (c g) -> p c g', g=G), AX.X, ALU.add).then_inc(s_psum_ready, 1)
            dve.wait_ge(s_psum_ready, up(cnt, "psum_ready"))
            b = sc_take()
            v.tensor_scalar(sc32[0:HPAIR, 0:NFREE], sc[0:HPAIR, b, 0:NFREE], 1.0, None, ALU.mult).then_inc(s_sc_free, 1)
            dve.wait_ge(s_sc_free, up(cnt, "sc_free"))
            s3 = sc32[0:HPAIR, 0:NFREE]
            r3, q3 = (a[0:HPAIR, :].rearrange("p (j i) -> p j i", j=NFREE) for a in (rank, rank2))
            v.tensor_tensor(r3, bc(s3, 1, NFREE), bc(s3, 2, NFREE), ALU.is_gt).then_inc(s_dve_step, 1)
            dve.wait_ge(s_dve_step, up(cnt, "dve_step"))
            v.tensor_tensor(q3, bc(s3, 1, NFREE), bc(s3, 2, NFREE), ALU.is_equal).then_inc(s_dve_step, 1)
            dve.wait_ge(s_dve_step, up(cnt, "dve_step"))
            v.tensor_tensor(q3, q3, C('tie').rearrange('p (j i) -> p j i', j=NFREE), ALU.mult).then_inc(s_dve_step, 1)
            dve.wait_ge(s_dve_step, up(cnt, "dve_step"))
            v.tensor_tensor(r3, r3, q3, ALU.add).then_inc(s_dve_step, 1)
            dve.wait_ge(s_dve_step, up(cnt, "dve_step"))
            v.memset(selm[0:HPAIR, :], 1.0).then_inc(s_dve_step, 1)
            dve.wait_ge(s_dve_step, up(cnt, "dve_step"))
            v.tensor_reduce(sc32[0:HPAIR, 0:NFREE], r3, AX.X, ALU.add).then_inc(s_dve_step, 1)
            dve.wait_ge(s_dve_step, up(cnt, "dve_step"))
            v.tensor_scalar(selm[0:HPAIR, 1:1 + NFREE], sc32[0:HPAIR, 0:NFREE], float(NPICK), None, ALU.is_lt).then_inc(s_chosen, 1)
            dve.wait_ge(s_chosen, up(cnt, "chosen"))
            b = sc_take()
            v.tensor_scalar(selT[0:NSB, :], sc[0:NSB, b, 0:HPAIR], 1.0, None, ALU.mult).then_inc(s_sc_free, 1)
            dve.wait_ge(s_sc_free, up(cnt, "sc_free"))
            dve.drain().then_inc(s_chosen, 1)
            up(cnt, "chosen")
            b = sc_take()
            v.tensor_scalar(mask32, sc[:, b, 0:HPAIR], -1.0, BIG, ALU.add, ALU.mult).then_inc(s_sc_free, 1)
            dve.wait_ge(s_sc_free, up(cnt, "sc_free"))
            blocks("cmpv", 2, value_block, 8, per)
            add_branch(0)

            with rounds_of(dve, cnt, 4, {"sc_ready": 2, "sc_free": 2}) as i:
                for bb in range(2):
                    b = sc_take()
                    v.tensor_scalar(S[:, ds(i * (2 * CS * NH) + bb * CS * NH, CS * NH)], sc[:, b, 0:CS * NH], 1.0, None, ALU.mult).then_inc(s_sc_free, 1)
                    dve.wait_ge(s_sc_free, up(cnt, "sc_free"))
            for bb in range(DB):
                x = S[:, bb * CS * NH:(bb + 1) * CS * NH].rearrange("p (t h g) -> p t h g", t=CS, h=NKV)
                m = mask32[:, bb * NKV:(bb + 1) * NKV].unsqueeze(1).unsqueeze(3).to_broadcast([128, CS, NKV, G])
                v.tensor_tensor(x, x, m, ALU.add).then_inc(s_dve_step, 1)
                dve.wait_ge(s_dve_step, up(cnt, "dve_step"))
            b = sc_take()
            v.tensor_tensor(SX[0:DB, :], sc[0:DB, b, 0:NC12], C('own'), ALU.add).then_inc(s_sc_free, 1)
            dve.wait_ge(s_sc_free, up(cnt, "sc_free"))
            sample_softmax(128, CS, NH, extra=True)
            with rounds_of(dve, cnt, 4, {"sc_ready": 2, "sc_free": 2}) as i:
                for bb in range(2):
                    b = sc_take()
                    v.tensor_scalar(OO[:, ds(i * (2 * NH) + bb * NH, NH)], sc[:, b, 0:NH], 1.0, None, ALU.mult).then_inc(s_sc_free, 1)
                    dve.wait_ge(s_sc_free, up(cnt, "sc_free"))
            b = sc_take()
            v.tensor_tensor(OO, OO, sc[:, b, 0:NC12], ALU.add).then_inc(s_sc_free, 1)
            dve.wait_ge(s_sc_free, up(cnt, "sc_free"))
            add_branch(1)

            for s in range(NS):
                b = sc_take()
                v.tensor_scalar(S[:, s * 8 * NH:(s + 1) * 8 * NH], sc[:, b, 0:8 * NH], 1.0, None, ALU.mult).then_inc(s_sc_free, 1)
                dve.wait_ge(s_sc_free, up(cnt, "sc_free"))
            sample_softmax(128, 4, NH)
            b = sc_take()
            v.tensor_scalar(OO, sc[:, b, 0:NC12], 1.0, None, ALU.mult).then_inc(s_sc_free, 1)
            dve.wait_ge(s_sc_free, up(cnt, "sc_free"))
            add_branch(2)
            v.tensor_scalar(u[:, 0:NH, SEQ:T], zacc[:, :].rearrange('p (b c) -> p c b', b=DB), 1.0, None, ALU.mult).then_inc(s_dve_step, 1)
            dve.wait_ge(s_dve_step, up(cnt, "dve_step"))
            sample_memory()
            dve.drain().then_inc(s_mixed, 1)
            up(cnt, "mixed")
            residual("out1", 1)
            ffn(1)
            norm(xT[:, :, :], T, GFIN)


_NAMES = ["x_prompt", "x_sample", "mem_prompt", "state_pool", "cache_cmp_kv", "cache_slc_kv", "cache_win_kv",
          "cache_mem_kv", "page_table", "g_mix", "w_in_a", "pool_grp_w", "pool_scale", "w_in_b", "b_gate", "g_kv",
          "w_kv", "cmp_pe", "cmp_w1", "cmp_w2", "g_mem", "w_mem_kv", "w_out", "g_ffn", "w_gu", "w_down", "g_final"]
_ROW = (2, NKV, HD)
_OUTS = [("y_p", (1, SEQ, D)), ("y_s", (DB, 1, D)), ("pool_p", (1, 1, PBUF, MAIN)), ("cmp_p", (1, SEQ) + _ROW),
         ("slc_p", (1, SEQ) + _ROW), ("win_p", (1, SEQ) + _ROW), ("mem", (2, 1, MEM) + _ROW),
         ("pool_s", (1, DB, PBUF, MAIN)), ("cmp_s", (DB, 1) + _ROW), ("slc_s", (DB, 1) + _ROW), ("win_s", (DB, WIN) + _ROW)]


def kernel(**inputs):
    import concourse.bacc as _bacc
    from concourse.bass_utils import run_bass_kernel_spmd as _run

    nc = _bacc.Bacc("TRN2", target_bir_lowering=False, num_devices=1)
    con, coff = constants()
    arrays = {f"in_{k}": np.ascontiguousarray(inputs[k]) for k in _NAMES}
    arrays["in_con"] = con
    inp = {k[3:]: nc.dram_tensor(k, a.shape, mybir.dt.from_np(a.dtype), kind="ExternalInput").ap() for k, a in arrays.items()}
    out = {k: nc.dram_tensor(f"out_{i}", s, mybir.dt.float32, kind="ExternalOutput").ap() for i, (k, s) in enumerate(_OUTS)}
    trunk_program(nc, inp, out, coff)
    r = _run(nc, [arrays], core_ids=[0])
    return tuple(r.results[0][f"out_{i}"] for i in range(len(_OUTS)))
```
